# Optimizing a Trainium2 kernel written in Bass

```python
import math
import functools
import jax
import jax.numpy as jnp
from jax import lax
import numpy as np

D_MODEL = 1024
BATCH = 1
SEQ = 2048
DEPTH = 1
DEC_BATCH = 8
DEC_SEQ = 8
PAST_LEN = 4096
PAGE_SIZE = 128

N_MIXERS = 4
W_GRP = D_MODEL // N_MIXERS
D_IN = 9 * W_GRP
LRU_HEADS = 4
LRU_HD = W_GRP // LRU_HEADS
LRU_CONV = 4
LRU_C = 8.0
SCONV_W = 3
S5_CH = 16
S5_GROUPS = W_GRP // S5_CH
S5_STATE = 64
ATT_HEADS = 4
HEAD_DIM = W_GRP // ATT_HEADS
PATTERNS = ((128, 1), (512, 4), (2048, 16))
MAX_WINDOW = 2048
Q_BLK = 128
REL_BUCKETS = 32
REL_MAX_DIST = 2048
N_GROUPS = 4
EXP_PER_GROUP = 8
N_EXPERTS = N_GROUPS * EXP_PER_GROUP
TOP_K = 2
D_EXPERT = 512
MOE_BLK = 128
EPS = 1e-6
NEG = -1e30

kernel_name = 'hybrid_parallel_groups_decode_step'

def _rms(x, g):
    xf = x.astype(jnp.float32)
    return xf * lax.rsqrt(jnp.mean(xf * xf, axis=-1, keepdims=True) + EPS) * g.astype(jnp.float32)

def _causal_conv(x, buf, w):
    K = w.shape[0]
    L = x.shape[1]
    xp = jnp.concatenate([buf.astype(x.dtype), x], axis=1)
    y = xp[:, 0:L] * w[0]
    for j in range(1, K):
        y = y + xp[:, j:j + L] * w[j]
    return y, xp[:, xp.shape[1] - (K - 1):]

def _lin_combine(e1, e2):
    a1, b1 = e1
    a2, b2 = e2
    return a1 * a2, a2 * b1 + b2

def _cplx_combine(e1, e2):
    ar1, ai1, br1, bi1 = e1
    ar2, ai2, br2, bi2 = e2
    return (ar1 * ar2 - ai1 * ai2, ar1 * ai2 + ai1 * ar2,
            ar2 * br1 - ai2 * bi1 + br2, ar2 * bi1 + ai2 * br1 + bi2)

def _rglru(x, h0, wa, ba, wx, bx, lam):
    f32 = jnp.float32
    Bn, L, W = x.shape
    xf = x.astype(f32)
    xh = xf.reshape(Bn, L, LRU_HEADS, LRU_HD)
    r = jax.nn.sigmoid(jnp.einsum('blhi,hij->blhj', xh, wa.astype(f32)).reshape(Bn, L, W) + ba.astype(f32))
    ig = jax.nn.sigmoid(jnp.einsum('blhi,hij->blhj', xh, wx.astype(f32)).reshape(Bn, L, W) + bx.astype(f32))
    log_a = -LRU_C * r * jax.nn.softplus(-lam.astype(f32))
    a = jnp.exp(log_a)
    b = jnp.sqrt(-jnp.expm1(2.0 * log_a)) * (ig * xf)
    b = b.at[:, 0].add(a[:, 0] * h0.astype(f32))
    _, h = lax.associative_scan(_lin_combine, (a, b), axis=1)
    return h, h[:, -1]

def _s5(u, h0r, h0i, p):
    f32 = jnp.float32
    Bn, L, W = u.shape
    uf = u.astype(f32)
    ug = uf.reshape(Bn, L, S5_GROUPS, S5_CH)
    step = jnp.exp(p['s5_log_dt'].astype(f32))[:, None]
    ar = p['s5_a_re'].astype(f32)
    ai = p['s5_a_im'].astype(f32)
    mag = jnp.exp(ar * step)
    ang = ai * step
    abr = mag * jnp.cos(ang)
    abi = mag * jnp.sin(ang)
    den = ar * ar + ai * ai
    zr = ((abr - 1.0) * ar + abi * ai) / den
    zi = (abi * ar - (abr - 1.0) * ai) / den
    b_re = p['s5_b_re'].astype(f32)
    b_im = p['s5_b_im'].astype(f32)
    bbr = zr[..., None] * b_re - zi[..., None] * b_im
    bbi = zr[..., None] * b_im + zi[..., None] * b_re
    bur = jnp.einsum('blgc,gpc->blgp', ug, bbr)
    bui = jnp.einsum('blgc,gpc->blgp', ug, bbi)
    h0r = h0r.astype(f32)
    h0i = h0i.astype(f32)
    bur = bur.at[:, 0].add(abr * h0r - abi * h0i)
    bui = bui.at[:, 0].add(abr * h0i + abi * h0r)
    are = jnp.broadcast_to(abr, bur.shape)
    aim = jnp.broadcast_to(abi, bur.shape)
    _, _, hr, hi = lax.associative_scan(_cplx_combine, (are, aim, bur, bui), axis=1)
    y = (jnp.einsum('blgp,gcp->blgc', hr, p['s5_c_re'].astype(f32))
         - jnp.einsum('blgp,gcp->blgc', hi, p['s5_c_im'].astype(f32))).reshape(Bn, L, W) + p['s5_d'].astype(f32) * uf
    g = jax.nn.gelu(y) @ p['s5_glu_w'].astype(f32) + p['s5_glu_b'].astype(f32)
    out = g[..., :W] * jax.nn.sigmoid(g[..., W:])
    return out, hr[:, -1], hi[:, -1]

def _t5_bucket(n):
    n = np.asarray(n).astype(np.int32)
    max_exact = REL_BUCKETS // 2
    nf = np.maximum(n, 1).astype(np.float32)
    large = max_exact + (np.log(nf / max_exact) / np.log(REL_MAX_DIST / max_exact)
                         * (REL_BUCKETS - max_exact)).astype(np.int32)
    large = np.minimum(large, REL_BUCKETS - 1)
    return np.where(n < max_exact, n, large).astype(np.int32)

def _head_prep(q, k, v, qn, kn):
    Bn, L, _ = q.shape
    q = _rms(q.reshape(Bn, L, ATT_HEADS, HEAD_DIM), qn) * (HEAD_DIM ** -0.5)
    k = _rms(k.reshape(Bn, L, ATT_HEADS, HEAD_DIM), kn)
    v = v.reshape(Bn, L, ATT_HEADS, HEAD_DIM).astype(jnp.float32)
    return q, k, v

def _merge_patterns(outs, lses):
    wts = jax.nn.softmax(jnp.stack(lses, axis=0), axis=0)
    return jnp.sum(wts[..., None] * jnp.stack(outs, axis=0), axis=0)

def _dilated_prompt_one(q, k, v, win, dil, rel_bias):
    Bn, L, H, E = q.shape
    span = win // dil
    md = L // dil
    nb = -(-md // Q_BLK)
    mp = nb * Q_BLK

    def to_res(t, front):
        t = t.reshape(Bn, md, dil, H, E).transpose(0, 2, 1, 3, 4)
        return jnp.pad(t, ((0, 0), (0, 0), (front, mp - md), (0, 0), (0, 0)))

    qb = to_res(q, 0).reshape(Bn, dil, nb, Q_BLK, H, E)
    kb = to_res(k, Q_BLK).reshape(Bn, dil, nb + 1, Q_BLK, H, E)
    vb = to_res(v, Q_BLK).reshape(Bn, dil, nb + 1, Q_BLK, H, E)
    kw = jnp.concatenate([kb[:, :, :-1], kb[:, :, 1:]], axis=3)
    vw = jnp.concatenate([vb[:, :, :-1], vb[:, :, 1:]], axis=3)
    i = np.arange(Q_BLK)[:, None]
    j = np.arange(2 * Q_BLK)[None, :]
    rel = Q_BLK + i - j
    key_m = np.arange(nb)[:, None, None] * Q_BLK - Q_BLK + j[None]
    mask = ((rel >= 0) & (rel <= span))[None] & (key_m >= 0)
    bias = rel_bias.astype(jnp.float32)[_t5_bucket(np.clip(rel, 0, None) * dil)].transpose(2, 0, 1)
    s = jnp.einsum('brnqhe,brnkhe->brnhqk', qb, kw) + bias
    s = jnp.where(mask[None, None, :, None], s, NEG)
    m = jnp.max(s, axis=-1, keepdims=True)
    pr = jnp.exp(s - m)
    den = jnp.sum(pr, axis=-1)
    o = jnp.einsum('brnhqk,brnkhe->brnqhe', pr, vw) / jnp.swapaxes(den, -1, -2)[..., None]
    lse = jnp.swapaxes(m[..., 0] + jnp.log(den), -1, -2)
    o = o.reshape(Bn, dil, mp, H, E)[:, :, :md].transpose(0, 2, 1, 3, 4).reshape(Bn, L, H, E)
    lse = lse.reshape(Bn, dil, mp, H)[:, :, :md].transpose(0, 2, 1, 3).reshape(Bn, L, H)
    return o, lse

def _attn_prompt(q, k, v, qn, kn, rel_bias):
    Bn, L, W = q.shape
    q, k, v = _head_prep(q, k, v, qn, kn)
    outs, lses = [], []
    for win, dil in PATTERNS:
        o, lse = _dilated_prompt_one(q, k, v, win, dil, rel_bias)
        outs.append(o)
        lses.append(lse)
    return _merge_patterns(outs, lses).reshape(Bn, L, W), k, v

def _dilated_sample_one(q, kall, vall, wb, win, dil, rel_bias):
    S = q.shape[1]
    span = win // dil
    kk = np.arange(span + 1)
    idx = wb + np.arange(S)[:, None] - kk[None, :] * dil
    valid = idx >= 0
    idxc = np.maximum(idx, 0)
    kg = kall[:, idxc]
    vg = vall[:, idxc]
    bias = rel_bias.astype(jnp.float32)[_t5_bucket(kk * dil)].T[:, None, :]
    s = jnp.einsum('bshe,bskhe->bhsk', q, kg) + bias
    s = jnp.where(valid[None, None], s, NEG)
    m = jnp.max(s, axis=-1, keepdims=True)
    pr = jnp.exp(s - m)
    den = jnp.sum(pr, axis=-1)
    o = jnp.einsum('bhsk,bskhe->bshe', pr, vg) / jnp.transpose(den, (0, 2, 1))[..., None]
    lse = jnp.transpose(m[..., 0] + jnp.log(den), (0, 2, 1))
    return o, lse

def _attn_sample(q, k, v, qn, kn, rel_bias, buf_k, buf_v):
    Bn, S, W = q.shape
    q, k, v = _head_prep(q, k, v, qn, kn)
    wb = buf_k.shape[1]
    kall = jnp.concatenate([buf_k.astype(jnp.float32), k], axis=1)
    vall = jnp.concatenate([buf_v.astype(jnp.float32), v], axis=1)
    outs, lses = [], []
    for win, dil in PATTERNS:
        o, lse = _dilated_sample_one(q, kall, vall, wb, win, dil, rel_bias)
        outs.append(o)
        lses.append(lse)
    return _merge_patterns(outs, lses).reshape(Bn, S, W), k, v

def _moe(h, p):
    f32 = jnp.float32
    Bn, L, D = h.shape
    T = Bn * L
    hf = h.reshape(T, D)
    g_logits = hf.astype(f32) @ p['router_g_w'].astype(f32) + p['router_g_b'].astype(f32)
    g_sel = jnp.argmax(g_logits, axis=-1).astype(jnp.int32)
    g_prob = jnp.take_along_axis(jax.nn.softmax(g_logits, axis=-1), g_sel[:, None], axis=1)
    e_logits = (hf.astype(f32) @ p['router_e_w'].astype(f32) + p['router_e_b'].astype(f32)).reshape(T, N_GROUPS, EXP_PER_GROUP)
    e_in = jnp.take_along_axis(e_logits, g_sel[:, None, None], axis=1)[:, 0]
    top_v, top_i = lax.top_k(e_in, TOP_K)
    gates = jax.nn.softmax(top_v, axis=-1) * g_prob
    ex = (g_sel[:, None] * EXP_PER_GROUP + top_i).reshape(-1).astype(jnp.int32)
    n_assign = T * TOP_K
    tok = jnp.repeat(jnp.arange(T, dtype=jnp.int32), TOP_K)
    wts = gates.reshape(-1)
    onehot = (ex[:, None] == jnp.arange(N_EXPERTS, dtype=jnp.int32)[None, :]).astype(jnp.int32)
    rank = jnp.take_along_axis(jnp.cumsum(onehot, axis=0), ex[:, None], axis=1)[:, 0] - 1
    counts = jnp.sum(onehot, axis=0)
    padded = (counts + MOE_BLK - 1) // MOE_BLK * MOE_BLK
    ends = jnp.cumsum(padded)
    dest = (ends - padded)[ex] + rank
    n_blk = -(-n_assign // MOE_BLK) + N_EXPERTS
    slot_tok = jnp.full((n_blk * MOE_BLK,), T, jnp.int32).at[dest].set(tok)
    slot_w = jnp.zeros((n_blk * MOE_BLK,), f32).at[dest].set(wts)
    blk_e = jnp.minimum(jnp.searchsorted(ends, jnp.arange(n_blk, dtype=jnp.int32) * MOE_BLK, side='right'), N_EXPERTS - 1)
    h_pad = jnp.concatenate([hf, jnp.zeros((1, D), hf.dtype)], axis=0)
    wg, wu, wd = p['moe_w_gate'], p['moe_w_up'], p['moe_w_down']

    def expert_block(args):
        ids, e = args
        xb = h_pad[ids]
        return (jax.nn.silu(xb @ wg[e]) * (xb @ wu[e])) @ wd[e]

    out = lax.map(expert_block, (slot_tok.reshape(n_blk, MOE_BLK), blk_e))
    y = jnp.zeros((T + 1, D), f32).at[slot_tok].add(out.reshape(-1, D).astype(f32) * slot_w[:, None])
    return y[:T].reshape(Bn, L, D)

def _layer(x, c, st, p, attn_fn):
    f32 = jnp.float32
    Bn, L, D = x.shape
    dt = x.dtype
    mod = jax.nn.silu(c.astype(f32)) @ p['mod_w'].astype(f32) + p['mod_b'].astype(f32)
    sh1, sc1, g1, sh2, sc2, g2 = [t[:, None, :] for t in jnp.split(mod, 6, axis=-1)]
    h = (_rms(x, p['norm_mix']) * (1.0 + sc1) + sh1).astype(dt)
    z = h @ p['w_in']
    xa, ga, gb, gc, xb, uc, q, k, v = jnp.split(z, 9, axis=-1)
    xa_conv, lru_conv_new = _causal_conv(xa, st['lru_conv'], p['lru_conv_w'])
    ha, lru_h_new = _rglru(xa_conv + p['lru_conv_b'], st['lru_h'], p['lru_wa'], p['lru_ba'],
                           p['lru_wx'], p['lru_bx'], p['lru_lambda'])
    out_a = ha * jax.nn.gelu(ga.astype(f32))
    yb, sconv_new = _causal_conv(gc * xb, st['sconv'], p['sconv_w'])
    out_b = (gb * yb).astype(f32)
    out_c, s5_re_new, s5_im_new = _s5(uc, st['s5_re'], st['s5_im'], p)
    out_d, k_rows, v_rows = attn_fn(q, k, v, p['q_norm'], p['k_norm'])
    mix = jnp.concatenate([out_a, out_b, out_c, out_d], axis=-1).reshape(Bn, L, N_MIXERS, W_GRP)
    mix = (mix * lax.rsqrt(jnp.mean(mix * mix, axis=-1, keepdims=True) + EPS)).reshape(Bn, L, D) * p['out_norm'].astype(f32)
    x = x + (g1 * (mix.astype(dt) @ p['w_out'])).astype(dt)
    h2 = (_rms(x, p['norm_ffn']) * (1.0 + sc2) + sh2).astype(dt)
    x = x + (g2 * _moe(h2, p)).astype(dt)
    new_st = {'lru_h': lru_h_new, 'lru_conv': lru_conv_new, 'sconv': sconv_new,
              's5_re': s5_re_new, 's5_im': s5_im_new, 'win_k': k_rows, 'win_v': v_rows}
    return x, new_st

def setup_inputs(seed: int = 0) -> dict:
    key = jax.random.key(seed)
    ks = iter(jax.random.split(key, 64))

    def nrm(shape, scale):
        return jax.random.normal(next(ks), shape, jnp.float32) * scale

    def gain(shape):
        return 1.0 + nrm(shape, 0.01)

    wb = min(MAX_WINDOW, PAST_LEN)
    lam_u = jax.random.uniform(next(ks), (DEPTH, W_GRP), jnp.float32, 0.9, 0.999)
    lam_s = lam_u ** (1.0 / LRU_C)
    n_idx = jnp.arange(S5_STATE, dtype=jnp.float32)
    return {
        'x_prompt': nrm((BATCH, SEQ, D_MODEL), 1.0),
        'x_sample': nrm((DEC_BATCH, DEC_SEQ, D_MODEL), 1.0),
        'c_prompt': nrm((BATCH, D_MODEL), 1.0),
        'c_sample': nrm((DEC_BATCH, D_MODEL), 1.0),
        'state_lru_h': nrm((DEPTH, DEC_BATCH, W_GRP), 0.5),
        'state_lru_conv': nrm((DEPTH, DEC_BATCH, LRU_CONV - 1, W_GRP), 1.0),
        'state_sconv': nrm((DEPTH, DEC_BATCH, SCONV_W - 1, W_GRP), 1.0),
        'state_s5_re': nrm((DEPTH, DEC_BATCH, S5_GROUPS, S5_STATE), 0.3),
        'state_s5_im': nrm((DEPTH, DEC_BATCH, S5_GROUPS, S5_STATE), 0.3),
        'cache_win_k': nrm((DEPTH, DEC_BATCH, wb, ATT_HEADS, HEAD_DIM), 1.0),
        'cache_win_v': nrm((DEPTH, DEC_BATCH, wb, ATT_HEADS, HEAD_DIM), 1.0),
        'rel_bias': nrm((REL_BUCKETS, ATT_HEADS), 0.5),
        'mod_w': nrm((DEPTH, D_MODEL, 6 * D_MODEL), 0.5 * D_MODEL ** -0.5),
        'mod_b': nrm((DEPTH, 6 * D_MODEL), 0.02),
        'norm_mix': gain((DEPTH, D_MODEL)),
        'norm_ffn': gain((DEPTH, D_MODEL)),
        'w_in': nrm((DEPTH, D_MODEL, D_IN), D_MODEL ** -0.5),
        'lru_conv_w': nrm((DEPTH, LRU_CONV, W_GRP), LRU_CONV ** -0.5),
        'lru_conv_b': nrm((DEPTH, W_GRP), 0.02),
        'lru_wa': nrm((DEPTH, LRU_HEADS, LRU_HD, LRU_HD), LRU_HD ** -0.5),
        'lru_ba': nrm((DEPTH, W_GRP), 0.02),
        'lru_wx': nrm((DEPTH, LRU_HEADS, LRU_HD, LRU_HD), LRU_HD ** -0.5),
        'lru_bx': nrm((DEPTH, W_GRP), 0.02),
        'lru_lambda': jnp.log(lam_s) - jnp.log1p(-lam_s),
        'sconv_w': nrm((DEPTH, SCONV_W, W_GRP), SCONV_W ** -0.5),
        's5_log_dt': jax.random.uniform(next(ks), (DEPTH, S5_GROUPS), jnp.float32, math.log(0.001), math.log(0.1)),
        's5_a_re': -0.5 + nrm((DEPTH, S5_GROUPS, S5_STATE), 0.01),
        's5_a_im': jnp.pi * n_idx + nrm((DEPTH, S5_GROUPS, S5_STATE), 0.01),
        's5_b_re': nrm((DEPTH, S5_GROUPS, S5_STATE, S5_CH), S5_CH ** -0.5),
        's5_b_im': nrm((DEPTH, S5_GROUPS, S5_STATE, S5_CH), S5_CH ** -0.5),
        's5_c_re': nrm((DEPTH, S5_GROUPS, S5_CH, S5_STATE), S5_STATE ** -0.5),
        's5_c_im': nrm((DEPTH, S5_GROUPS, S5_CH, S5_STATE), S5_STATE ** -0.5),
        's5_d': nrm((DEPTH, W_GRP), 1.0),
        's5_glu_w': nrm((DEPTH, W_GRP, 2 * W_GRP), W_GRP ** -0.5),
        's5_glu_b': nrm((DEPTH, 2 * W_GRP), 0.02),
        'q_norm': gain((DEPTH, HEAD_DIM)),
        'k_norm': gain((DEPTH, HEAD_DIM)),
        'out_norm': gain((DEPTH, D_MODEL)),
        'w_out': nrm((DEPTH, D_MODEL, D_MODEL), D_MODEL ** -0.5),
        'router_g_w': nrm((DEPTH, D_MODEL, N_GROUPS), D_MODEL ** -0.5),
        'router_g_b': nrm((DEPTH, N_GROUPS), 0.01),
        'router_e_w': nrm((DEPTH, D_MODEL, N_EXPERTS), D_MODEL ** -0.5),
        'router_e_b': nrm((DEPTH, N_EXPERTS), 0.01),
        'moe_w_gate': nrm((DEPTH, N_EXPERTS, D_MODEL, D_EXPERT), D_MODEL ** -0.5),
        'moe_w_up': nrm((DEPTH, N_EXPERTS, D_MODEL, D_EXPERT), D_MODEL ** -0.5),
        'moe_w_down': nrm((DEPTH, N_EXPERTS, D_EXPERT, D_MODEL), D_EXPERT ** -0.5),
    }

def reference(x_prompt, x_sample, c_prompt, c_sample, state_lru_h, state_lru_conv, state_sconv, state_s5_re, state_s5_im,
              cache_win_k, cache_win_v, rel_bias, mod_w, mod_b, norm_mix, norm_ffn, w_in, lru_conv_w, lru_conv_b,
              lru_wa, lru_ba, lru_wx, lru_bx, lru_lambda, sconv_w, s5_log_dt, s5_a_re, s5_a_im, s5_b_re, s5_b_im,
              s5_c_re, s5_c_im, s5_d, s5_glu_w, s5_glu_b, q_norm, k_norm, out_norm, w_out, router_g_w, router_g_b,
              router_e_w, router_e_b, moe_w_gate, moe_w_up, moe_w_down):
    Bp, L, _ = x_prompt.shape
    dt = x_prompt.dtype
    wp = min(MAX_WINDOW, L)
    names = ('lru_h', 'lru_conv', 'sconv', 's5_re', 's5_im', 'win_k', 'win_v')
    acc_p = {n: [] for n in names}
    acc_s = {n: [] for n in names}
    xp, xs = x_prompt, x_sample
    for l in range(DEPTH):
        p = {'mod_w': mod_w[l], 'mod_b': mod_b[l], 'norm_mix': norm_mix[l], 'norm_ffn': norm_ffn[l], 'w_in': w_in[l],
             'lru_conv_w': lru_conv_w[l], 'lru_conv_b': lru_conv_b[l], 'lru_wa': lru_wa[l], 'lru_ba': lru_ba[l],
             'lru_wx': lru_wx[l], 'lru_bx': lru_bx[l], 'lru_lambda': lru_lambda[l], 'sconv_w': sconv_w[l],
             's5_log_dt': s5_log_dt[l], 's5_a_re': s5_a_re[l], 's5_a_im': s5_a_im[l], 's5_b_re': s5_b_re[l],
             's5_b_im': s5_b_im[l], 's5_c_re': s5_c_re[l], 's5_c_im': s5_c_im[l], 's5_d': s5_d[l],
             's5_glu_w': s5_glu_w[l], 's5_glu_b': s5_glu_b[l], 'q_norm': q_norm[l], 'k_norm': k_norm[l],
             'out_norm': out_norm[l], 'w_out': w_out[l], 'router_g_w': router_g_w[l], 'router_g_b': router_g_b[l],
             'router_e_w': router_e_w[l], 'router_e_b': router_e_b[l], 'moe_w_gate': moe_w_gate[l],
             'moe_w_up': moe_w_up[l], 'moe_w_down': moe_w_down[l]}
        zero_st = {'lru_h': jnp.zeros((Bp, W_GRP), dt),
                   'lru_conv': jnp.zeros((Bp, LRU_CONV - 1, W_GRP), dt),
                   'sconv': jnp.zeros((Bp, SCONV_W - 1, W_GRP), dt),
                   's5_re': jnp.zeros((Bp, S5_GROUPS, S5_STATE), dt),
                   's5_im': jnp.zeros((Bp, S5_GROUPS, S5_STATE), dt)}
        xp, stp = _layer(xp, c_prompt, zero_st, p, functools.partial(_attn_prompt, rel_bias=rel_bias))
        stp['win_k'] = stp['win_k'][:, L - wp:]
        stp['win_v'] = stp['win_v'][:, L - wp:]
        samp_st = {'lru_h': state_lru_h[l], 'lru_conv': state_lru_conv[l], 'sconv': state_sconv[l],
                   's5_re': state_s5_re[l], 's5_im': state_s5_im[l]}
        xs, sts = _layer(xs, c_sample, samp_st, p,
                         functools.partial(_attn_sample, rel_bias=rel_bias, buf_k=cache_win_k[l], buf_v=cache_win_v[l]))
        for n in names:
            acc_p[n].append(stp[n])
            acc_s[n].append(sts[n])
    new_p = {n: jnp.stack(acc_p[n], axis=0) for n in names}
    new_s = {n: jnp.stack(acc_s[n], axis=0) for n in names}
    return (xp, xs,
            new_p['lru_h'], new_p['lru_conv'], new_p['sconv'], new_p['s5_re'], new_p['s5_im'], new_p['win_k'], new_p['win_v'],
            new_s['lru_h'], new_s['lru_conv'], new_s['sconv'], new_s['s5_re'], new_s['s5_im'], new_s['win_k'], new_s['win_v'])


_drawn_inputs = setup_inputs


def setup_inputs(seed=0):
    import zlib

    import numpy as np

    out = dict(_drawn_inputs(seed))
    spreads = {}
    factors = {'norm_mix': 3.705,
     'norm_ffn': 8.0,
     'lru_ba': 8.0,
     'lru_bx': 8.0,
     's5_a_re': 3.183,
     's5_glu_b': 6.409,
     'q_norm': 8.0,
     'k_norm': 5.508,
     'out_norm': 8.0,
     'router_g_b': 8.0,
     'router_e_b': 8.0}
    for name, (base, spread) in spreads.items():
        noise = np.random.default_rng([zlib.crc32(name.encode()), seed]).standard_normal(out[name].shape)
        drawn = base * np.exp(spread * noise) if base else spread * noise
        out[name] = jnp.asarray(drawn.astype(out[name].dtype))
    for name, factor in factors.items():
        out[name] = (out[name] * factor).astype(out[name].dtype)
    return out
```

```python
from contextlib import ExitStack

import numpy as np
import concourse.bass as bass
from concourse import mybir

F32 = mybir.dt.float32
I32 = mybir.dt.int32
ALU = mybir.AluOpType
ACT = mybir.ActivationFunctionType
AX = mybir.AxisListType

P = 128
D = 1024
KT = D // P
TP = 2048
NB, NS = 8, 8
T = TP + NB * NS
W = 256
NT = -(-T // P)
CHUNKS = [(c, min(512, T - c)) for c in range(0, T, 512)]
EPS = 1e-6
NEG = -1e30

G16, SC, CL = 16, 16, 8
NCP = TP // CL
NC = NCP + NB
GH = 8

XA, GA, GB, GC, XB, UC = range(6)
ZTILES = [(XA, 0), (XA, 1), (UC, 0), (UC, 1), (GA, 0), (GA, 1), (GC, 0), (GC, 1), (XB, 0), (XB, 1), (GB, 0), (GB, 1)]
ZINDEX = {t: i for i, t in enumerate(ZTILES)}

VCOLS = {}
_at = 0
for _n, _w in [("norm_mix", 8), ("conv_w", 8), ("conv_b", 2), ("ba", 2), ("bx", 2), ("lam", 2), ("sconv_w", 6),
               ("s5_d", 2), ("glu_b", 4), ("out_norm", 8), ("h0", 16), ("conv0", 48), ("sconv0", 32), ("sgn", 1)]:
    VCOLS[_n] = (_at, _w)
    _at += _w
NV = _at

BK = 32
QB = 128
L1 = 384
L2 = 640
L3 = 2064
GRP, EPG, NE = 4, 8, 32
MOEB = 256
NBLK = (2 * T + NE * (MOEB - 1)) // MOEB
NSUB = 2 * NBLK
NSLOT = NBLK * MOEB
LAST = NBLK // 2 - 1
assert NBLK % 2 == 0
DE = 512


FIRST = ["c_silu", "glu_done", "glu_gelu", "glu_y", "h_ready", "hs_ready", "ld_modw0", "ld_modw1",
         "ld_modw2", "ld_modw3", "ld_qkvw", "ld_s5", "ld_vec", "ld_gatew", "ld_wz0", "ld_wz1", "ld_wz2",
         "ld_x0", "ld_x1", "ld_x2", "ld_x3", "ld_x4", "lru_par", "lru_y", "lru_w", "lru_h", "lru_g", "mixer_done", "modT_mm",
         "modT_ready", "mod_mm", "mod_row", "mx_free0", "mx_free1", "mx_free2", "mx_free3", "mx_free4", "mx_full", "norm1_mm",
         "norm1_sq", "norm1_sqrt", "norm1_var", "norm1_x", "ones_ready", "out_normed", "out_sq", "out_sqrt", "out_var",
         "qk_ready", "qk_sq", "qk_sqrt", "qk_ss", "qkT_ready", "v_free", "v_mm", "s5_ang", "s5_et", "s5_ff", "s5_fin", "s5_g",
         "s5_h", "s5_kern", "s5_step", "s5_trig", "s5_y", "z_free", "z_mm"]
SECOND = ["att_exp", "att_max", "att_o", "att_pT", "att_ptA", "att_ptV", "att_pv", "att_s", "comb_done", "dest_ready", "g_mm",
          "h2T_mm", "h2T_ready", "h2_ready", "h2_stored", "hT_mm", "hT_ready", "h_ready2", "lg_free", "lg_mm", "mrg_d",
          "mrg_e", "mrg_o", "mrg_sqrt", "mrg_ss", "odT_mm", "odT_ready", "prj_free", "prj_mm", "qb_ready",
          "route_const", "route_done", "rt_e", "rt_mm", "rt_oh", "rt_x", "silu", "smp_exp", "smp_max", "smp_o", "smp_pT",
          "smp_pt", "smp_pv", "smp_s", "tok_copied", "u_mm", "x1_ready", "x1_sqrt", "x1_ss", "x1_var", "xT_mm", "xtA", "xtV",
          "yA", "yV", "y_mm", "tab_mm", "tab_done",
          "ld_cx0", "ld_cx1", "ld_cx2", "ld_cx3", "ld_g2", "st_out0", "st_out1",
          "st_out2", "st_out3"]
AGAIN = dict(zip(SECOND, FIRST))


def ring_plan(schedule, tiles):
    base, n = {}, 0
    for step in schedule:
        base[step] = n
        n += 0 if step == ("qkv", 0) else tiles.get(step[0], 0)
    return base


def build(nc, A, O):
    with ExitStack() as ctx:
        sems = {}

        def S(name):
            name = AGAIN.get(name, name)
            if name not in sems:
                sems[name] = ctx.enter_context(nc.semaphore(name))
            return sems[name]

        def linker(eng, name):
            count = [0]

            def link(ins):
                count[0] += 1
                ins.then_inc(S(name), 1)
                eng.wait_ge(S(name), count[0])
            return link

        arena = ctx.enter_context(nc.sbuf_tensor("arena", [P, 53200], F32))
        top = [0]

        def take(n, at=None):
            if at is None:
                at = top[0]
                top[0] += n
            assert at + n <= 53200, (at, n)
            return arena[:, at:at + n]

        bank = [ctx.enter_context(nc.psum_tensor(f"bank{i}", [P, 512], F32)) for i in range(8)]

        ident = take(P)
        ones = take(P)
        jmat = take(P)
        vec = take(NV)
        modT = take(16 * 9).rearrange("p (k b) -> p k b", b=9)
        sc1 = take(8 * 9).rearrange("p (k b) -> p k b", b=9)
        sm = take(400)

        def V(name, i=None):
            a, w = VCOLS[name]
            return vec[:, a:a + w] if i is None else vec[:, a + i:a + i + 1]

        gatew = take(4 * P).rearrange("p (n m) -> p n m", n=4)
        lg = take(NT * 36).rearrange("p (i n) -> p i n", i=NT)
        zero = lg.rearrange("p i n -> p (i n)")[:, 0:512]
        s5_at = top[0]
        s5p = take(16 * 16).rearrange("p (n g) -> p n g", n=16)
        s5b = take(4 * 256).rearrange("p (n g c) -> p n g c", n=4, g=16)
        pwr = take(9 * 16).rearrange("p (d g) -> p d g", g=16)
        pwi = take(9 * 16).rearrange("p (d g) -> p d g", g=16)
        rot = take(2 * 9 * 16).rearrange("p (r d g) -> p r d g", r=2, g=16)
        ff = take(GH * 9 * 16).rearrange("p (g d c) -> p g d c", g=GH, d=9)
        toep = take(GH * P).rearrange("p (g m) -> p g m", g=GH)
        emat = take(GH * P).rearrange("p (g m) -> p g m", g=GH)
        emat2 = take(GH * P).rearrange("p (g m) -> p g m", g=GH)
        hfin = take(272)
        hfin_p = hfin[:, 0:16]
        hfin_s = hfin[:, 16:144].rearrange("p (g b) -> p g b", g=16)

        h_at = top[0]
        hT = take(KT * T).rearrange("p (k t) -> p k t", k=KT)
        w_at = top[0]
        wz = take(3 * 1024).rearrange("p (n k m) -> p n k m", n=3, k=KT)
        zst = take(2 * T).rearrange("p (n t) -> p n t", n=2)
        m_at = top[0]
        BW = 2144
        buf = [take(BW) for _ in range(9)]
        m_end = top[0]
        wqkv = take(6144, w_at).rearrange("p (k n) -> p k n", k=KT)
        gain = take(512, w_at + 6144)
        qks = emat.rearrange("p g m -> p (g m)").rearrange("p (n c) -> p n c", n=2)
        vst = take(2 * 256).rearrange("p (n c) -> p n c", n=2)
        ksq = take(512, w_at + 6656)
        tst = take(512).rearrange("p (n c) -> p n c", n=4)
        kss = take(8)
        t1 = take(1024, s5_at).rearrange("p (h k) -> p h k", h=4)
        t2 = take(2048, s5_at + 1024).rearrange("p (h k) -> p h k", h=4)
        ts = take(2056, s5_at + 3072)
        assert s5_at + 3072 + 2056 <= h_at
        top[0] = h_at
        qkT = take(4 * T).rearrange("p (n t) -> p n t", n=4)
        v1 = take(4096).rearrange("p (b c) -> p b c", b=16)
        v2 = take(4096).rearrange("p (b c) -> p b c", b=16)
        ssb = take(2048).rearrange("p (n k) -> p n k", n=4)
        pp = take(2048).rearrange("p (n k) -> p n k", n=4)
        pt = take(2048).rearrange("p (n k) -> p n k", n=4)
        ost = take(2 * 264).rearrange("p (n h c) -> p n h c", n=2, h=4)
        nmax = take(4)
        kc = take(2 * 2560).rearrange("p (n h k) -> p n h k", n=2, h=2)
        vc = take(2 * 2560).rearrange("p (n k c) -> p n k c", n=2, k=10)
        vn = take(2048).rearrange("p (b c) -> p b c", b=NB)
        qb = take(512).rearrange("p (b n m) -> p b n m", b=NB, n=2)
        sss = take(1288)
        spp = take(1288)
        spt = take(11 * P).rearrange("p (n m) -> p n m", n=11)
        hsel = take(4)
        sov = take(256)
        so = take(64)
        sst = take(4)
        tabc = take(3088, h_at)
        tabs = take(3088, h_at + 3088)
        rbx = take(4, h_at + 2 * 3088)
        assert top[0] <= 53200
        top[0] = s5_at
        wo = take(8192).rearrange("p (k n) -> p k n", k=KT)
        rw = take(288).rearrange("p (k n) -> p k n", k=KT)
        rb = take(36)
        grow = [take(3072).rearrange("p (n d) -> p n d", n=3) for _ in range(2)]
        nrow = take(1024)
        mixl = take(3 * 768).rearrange("p (n k t) -> p n k t", n=3, k=6)
        ma = take(2 * 528).rearrange("p (n q h c) -> p n q h c", n=2, q=2, h=4)
        mw = take(48).rearrange("p (n h) -> p n h", n=12)
        od = take(2 * 256).rearrange("p (n c) -> p n c", n=2)
        odt = take(2 * 256).rearrange("p (n k t) -> p n k t", n=2, k=2)
        osq = take(256)
        xt = take(2 * 1024).rearrange("p (n d) -> p n d", n=2)
        x1 = take(2 * 1024).rearrange("p (n d) -> p n d", n=2)
        h2 = take(2 * 1024).rearrange("p (n d) -> p n d", n=2)
        h2T = take(2 * 1024).rearrange("p (n k t) -> p n k t", n=2, k=KT)
        xsq = take(1024)
        top[0] = s5_at
        wg = take(2 * 4096).rearrange("p (s k n) -> p s k n", s=2, k=KT)
        wu = take(2 * 4096).rearrange("p (s k n) -> p s k n", s=2, k=KT)
        wd = take(2 * 4096).rearrange("p (s k n) -> p s k n", s=2, k=4)
        xg = take(2 * 1024).rearrange("p (s d) -> p s d", s=2)
        xgT = take(2 * 1024).rearrange("p (s k t) -> p s k t", s=2, k=KT)
        gs = take(512)
        hh = take(512)
        hhT = take(512).rearrange("p (k t) -> p k t", k=4)
        yb = take(2 * 1024).rearrange("p (s d) -> p s d", s=2)
        dest = take(NT * 2).bitcast(I32).rearrange("p (i k) -> p i k", k=2)
        gate = take(NT * 2).rearrange("p (i k) -> p i k", k=2)
        tids = take(NT).bitcast(I32)
        toks = take(NSUB).bitcast(I32)
        tokc = take(2).bitcast(I32)
        bexp = take(NBLK).bitcast(I32)
        used = take(NSUB).bitcast(I32)
        zero_i = take(NSUB).bitcast(I32)
        rt = [take(NT * 32).rearrange("p (i e) -> p i e", i=NT) for _ in range(6)]
        rs = take(NT * 8 * 3).rearrange("p (n i e) -> p n i e", n=3, i=NT)
        re_ = take(32 * 6).rearrange("p (n e) -> p n e", n=6)
        io32 = take(32)
        tri = take(P)
        blk0 = take(NSUB)
        zsum = take(NSUB)
        assert top[0] <= 53200, top[0]
        io_i = rs.rearrange("p n i e -> p (n i e)")[:, 0:32].bitcast(I32)
        blk_i = rs.rearrange("p n i e -> p (n i e)")[:, 32:32 + NSUB].bitcast(I32)
        cmpb = take(NSUB * 32, s5_at).rearrange("p (b e) -> p b e", b=NSUB)
        cmpc = take(NSUB * 32, s5_at + NSUB * 32).rearrange("p (b e) -> p b e", b=NSUB)
        cy = take(4 * 2048, s5_at).rearrange("p (s k d) -> p s k d", s=4, k=2)
        cx = take(4 * 1024, s5_at + 8192).rearrange("p (s d) -> p s d", s=4)
        g2r = take(2048, s5_at + 8192 + 4096).rearrange("p (n d) -> p n d", n=2)
        modw = take(4 * 4096, h_at).rearrange("p (n k m) -> p n k m", n=4, k=KT)
        modrow = take(6144, m_at)
        modb = take(6144, m_at + 6144)
        cT = take(72, m_at + 2 * 6144).rearrange("p (k b) -> p k b", b=9)
        cS = take(72, m_at + 2 * 6144 + 72).rearrange("p (k b) -> p k b", b=9)
        sq1 = take(2 * 512, m_at).rearrange("p (n t) -> p n t", n=2)
        rst1 = take(512, m_at + 1024)

        def dram(name, shape, dt=F32):
            return nc.dram_tensor(name, shape, dt).ap()

        mod_d = dram("mod_d", (9, 6144))
        z_d = dram("z_d", (12, P, T))
        y5_d = dram("y5_d", (2, P, T))
        mix_d = dram("mix_d", (6, P, T))
        qkT_d = dram("qkT_d", (4, P, T))
        tab_d = dram("tab_d", (4, L1 + L2 + L3))
        sk1_d = dram("sk1_d", (4, P, L1))
        sk2_d = dram("sk2_d", (4, P, L2))
        sk3_d = dram("sk3_d", (4, NS, L3))
        att_d = dram("att_d", (2, TP, 264))
        smp_d = dram("smp_d", (NB, 4, NS, 64))
        x1_d = dram("x1_d", (T, D))
        h2_d = dram("h2_d", (T, D))
        tok_d = dram("tok_d", (NSLOT, 1), I32)
        ye_d = dram("ye_d", (NSLOT, D))

        SCHEDULE = [("mod",), ("s5par",), ("norm1",), ("z", 0), ("z", 1), ("z", 2), ("z", 3), ("z", 4),
                    ("A", 0), ("z", 5), ("A", 1), ("z", 6), ("outA",), ("z", 7), ("s5prep", 0), ("z", 8), ("s5", 0), ("z", 9),
                    ("s5prep", 1), ("z", 10), ("s5", 1), ("z", 11), ("qkv", 0), ("qkv", 1), ("B", 0), ("qkv", 2), ("qkv", 3), ("B", 1), ("qkv", 4), ("qkv", 5), ("qkv", 6),
                    ("outB",), ("qkv", 7), ("qkv", 8), ("qkv", 9), ("glu",), ("qkv", 10), ("qkv", 11), ("qkv", 12), ("outC",),
                    ("qkv", 13), ("qkv", 14), ("qkv", 15), ("qkv", 16), ("qkv", 17),
                    ("bar", 1), ("tab",), ("att",), ("smp",), ("bar", 2), ("rows",)]
        SCHEDULE += [("row", i) for i in range(NT + 3)]
        SCHEDULE += [("bar", 3), ("route",), ("moe",), ("bar", 4), ("comb",)]
        TILES = {"A": 10, "s5prep": 4, "s5": 16 + 4 + 1 + 8, "outA": 5, "outB": 5, "outC": 5, "glu": 20, "qkv": 1}
        base = ring_plan(SCHEDULE, TILES)
        RB = 5

        def mx(n):
            return bank[2 + n % RB][:, :]

        def mx_take(pe, n):
            if n >= RB:
                pe.wait_ge(S(f"mx_free{n % RB}"), n // RB)

        MIX = [s for s in SCHEDULE if s[0] in ("A", "B", "s5prep", "s5", "outA", "outB", "outC", "glu")]
        ORD = {s: i for i, s in enumerate(MIX)}
        OUTN = {s[0]: i + 1 for i, s in enumerate(s for s in MIX if s[0].startswith("out"))}
        ST_MIX, _n = {}, 0
        for s in MIX:
            _n += {"A": 64, "B": 32, "s5": 32}.get(s[0], 0)
            ST_MIX[s] = _n

        def run(steps):
            for step in SCHEDULE:
                f = steps.get(step[0])
                if f:
                    f(step, *step[1:])

        def parts(*steps):
            def f(step, i):
                for g, lag in steps:
                    if 0 <= i - lag < NT:
                        g(i - lag)
            return f

        def barrier(eng):
            def f(step, n):
                eng.sem_inc(S("phase"), 1)
                eng.wait_ge(S("phase"), 5 * n)
                if n == 1:
                    if eng is nc.sync:
                        for name in FIRST[:len(SECOND)]:
                            eng.sem_clear(S(name))
                        eng.drain().then_inc(S("cleared"), 1)
                    eng.wait_ge(S("cleared"), 1)
                    eng.sem_inc(S("second_part"), 1)
            return f

        def rows(i):
            return min(P, T - i * P)

        def flag(eng, b):
            return eng.value_load(used[0:1, bass.ds(b, 1)], min_val=0, max_val=1)

        def if_used(eng, u, work, signals):
            if u is None:
                work()
                return
            with eng.If(u > 0):
                work()
            with eng.Else():
                for name, before, n in signals:
                    if not (isinstance(before, int) and before == 0):
                        eng.wait_ge(S(name), before)
                    eng.sem_inc(S(name), n)

        def quads(eng, sub, signals):
            for q in range(4):
                sub(0, q, None if q == 0 or eng is nc.gpsimd else flag(eng, q))
            with eng.Fori(1, LAST) as it:
                four(eng, it, sub, signals)
            four(eng, LAST, sub, signals)

        def four(eng, it, sub, signals):
            def work():
                for q in range(4):
                    sub(it, q, None if q == 0 or eng is nc.gpsimd else flag(eng, it * 4 + q))
            if_used(eng, flag(eng, it * 4), work, signals(it))

        BLOCKS = []
        for n in range(TP // QB):
            k0 = max(n - 1, 0)
            BLOCKS.append((0, n, slice(n * QB, (n + 1) * QB), slice(k0 * QB, (n + 1) * QB), range(k0, n + 1)))
        for r in range(4):
            for n in range(4):
                BLOCKS.append((1, 4 * r + n, slice(r + 4 * QB * n, r + 4 * (QB * (n + 1) - 1) + 1, 4),
                               slice(r, r + 4 * (QB * (n + 1) - 1) + 1, 4), range(4 * r, 4 * r + n + 1)))
        NU = 4 * len(BLOCKS)

        block = ctx.enter_context(nc.Block())

        @block.sync
        def _(sp):
            def mod(step):
                sp.dma_start(vec, A["vec"]).then_inc(S("ld_vec"), 16)
                sp.dma_start(ident, A["ident"]).then_inc(S("ld_vec"), 16)
                sp.dma_start(jmat, A["jmat"]).then_inc(S("ld_vec"), 16)
                sp.dma_start(cT, A["cT"]).then_inc(S("ld_vec"), 16)
                sp.dma_start(modb[0:1, :], A["mod_b"]).then_inc(S("ld_vec"), 16)
                sp.dma_start(gatew, A["gatew"]).then_inc(S("ld_gatew"), 16)
                sp.dma_start(s5p[:, 0:3, :], A["s5p"]).then_inc(S("ld_s5"), 16)
                sp.dma_start(s5b, A["s5b"]).then_inc(S("ld_s5"), 16)
                for n in range(12):
                    if n >= 4:
                        sp.wait_ge(S("mod_mm"), n - 3)
                    sp.dma_start(modw[:, n % 4], A["mod_w"][n]).then_inc(S(f"ld_modw{n % 4}"), 16)

            def norm1(step):
                sp.wait_ge(S("mod_mm"), 12)
                for c, (t0, w) in enumerate(CHUNKS):
                    sp.dma_start(hT[:, :, t0:t0 + w], A["xT"][:, :, t0:t0 + w]).then_inc(S(f"ld_x{c}"), 16)

            def z(step, i):
                if i >= 3:
                    sp.wait_ge(S("z_mm"), 5 * (i - 2))
                sp.dma_start(wz[:, i % 3], A["w_z"][i]).then_inc(S(f"ld_wz{i % 3}"), 16)
                if i == 0:
                    sp.wait_ge(S("zero_ready"), 1)
                m = NSUB // 12
                dst = ye_d[i * m * P:(i + 1) * m * P].rearrange("(p n) (h d) -> p (n h) d", p=P, h=2)
                sp.dma_start(dst, zero.unsqueeze(1).broadcast_to([P, 2 * m, 512])).then_inc(S("st_zero_ye"), 16)

            def qkv(step, i):
                if i == 0:
                    sp.wait_ge(S("z_mm"), 60)
                    for q in range(2):
                        sp.wait_ge(S(f"z_stored{q}"), 16 * 6)
                    sp.dma_start(wqkv, A["w_qkv"]).then_inc(S("ld_qkvw"), 16)
                    sp.dma_start(gain, A["qk_gain"]).then_inc(S("ld_qkvw"), 16)
                if i:
                    r, t0 = rows(i - 1), (i - 1) * P
                    sp.wait_ge(S("qk_ready"), i)
                    sp.dma_start(O["k"][t0:t0 + r], qks[0:r, (i - 1) % 2, 256:512]).then_inc(S(f"st_k{(i - 1) % 2}"), 16)
                    sp.wait_ge(S("qkT_ready"), i)
                    sp.dma_start(qkT_d[:, :, t0:t0 + r].rearrange("n p t -> p n t"), tst[:, :, 0:r]).then_inc(S("st_qkT"), 16)

            def bar(step, n):
                if n == 1:
                    for q in range(2):
                        sp.wait_ge(S(f"st_k{q}"), 16 * (9 - q))
                    sp.wait_ge(S("st_qkT"), 16 * NT)
                    sp.wait_ge(S("st_zero_ye"), 16 * 12)
                barrier(sp)(step, n)

            def tab(step):
                sp.dma_start(tabc[0:33], A["tabc"]).then_inc(S("ld_tab"), 16)
                sp.dma_start(rbx[0:33], A["rbx"]).then_inc(S("ld_tab"), 16)
                sp.dma_start(v1, O["v"][0:TP].rearrange("(b p) c -> p b c", p=P)).then_inc(S("ld_v1"), 16)
                for r in range(4):
                    sp.dma_start(v2[:, 4 * r:4 * r + 4], O["v"][0:TP].rearrange("(b p r) c -> r p b c", p=P, r=4)[r]).then_inc(S("ld_v2"), 16)
                for b in range(NB):
                    sp.dma_start(vn[0:8, b], O["v"][TP + 8 * b:TP + 8 * b + 8]).then_inc(S("ld_vn"), 16)
                sp.dma_start(hsel, A["hsel"]).then_inc(S("ld_vn"), 16)
                sp.wait_ge(S("tab_done"), 1)
                sp.dma_start(tab_d, tabs[0:4]).then_inc(S("st_tab"), 16)
                sp.wait_ge(S("st_tab"), 16)
                for h in range(4):
                    row = tab_d[h:h + 1]
                    sp.dma_start(sk1_d[h], row[:, 0:L1].broadcast_to([P, L1])).then_inc(S("st_skew"), 16)
                    sp.dma_start(sk2_d[h], row[:, L1:L1 + L2].broadcast_to([P, L2])).then_inc(S("st_skew"), 16)
                    sp.dma_start(sk3_d[h], row[:, L1 + L2:].broadcast_to([8, L3])).then_inc(S("st_skew"), 16)
                sp.wait_ge(S("st_skew"), 16 * 12)
                for h in range(4):
                    sp.dma_start(t1[:, h, :], bass.AP(tensor=sk1_d.tensor, offset=h * P * L1 + 127, ap=[[L1 - 1, P], [1, 256]])).then_inc(S("ld_t1"), 16)
                    sp.dma_start(t2[:, h, :], bass.AP(tensor=sk2_d.tensor, offset=h * P * L2 + 127, ap=[[L2 - 1, P], [1, 512]])).then_inc(S("ld_t1"), 16)
                for b in range(4):
                    for h in range(4):
                        p0 = 32 * b + 8 * h
                        sp.dma_start(ts[p0:p0 + 8, :], bass.AP(tensor=sk3_d.tensor, offset=h * 8 * L3 + 7,
                                                               ap=[[L3 - 1, 8], [1, 2056]])).then_inc(S("ld_ts"), 16)
                sp.dma_start(qkT, qkT_d.rearrange("n p t -> p n t")).then_inc(S("ld_qkT"), 16)

            def att(step):
                for bk, (ps, n, q, k, vt) in enumerate(BLOCKS):
                    sp.wait_ge(S("att_o"), bk + 1)
                    dst = att_d[ps, q].rearrange("t (h c) -> t h c", h=4)
                    sp.dma_start(dst, ost[:, bk % 2]).then_inc(S(f"st_att{bk % 2}"), 16)

            def smp(step):
                for hf in range(2):
                    for b in range(4 * hf, 4 * hf + 4):
                        if b >= 2:
                            sp.wait_ge(S("smp_s"), b - 1)
                        sp.dma_start(kc[:, b % 2], A["kc"][b]).then_inc(S(f"ld_kc{b % 2}"), 16)
                    for b in range(4 * hf, 4 * hf + 4):
                        if b >= 2:
                            sp.wait_ge(S("smp_pv"), b - 1)
                        sp.dma_start(vc[:, b % 2], A["vc"][b]).then_inc(S(f"ld_vc{b % 2}"), 16)
                    sp.wait_ge(S("smp_o"), hf + 1)
                    sp.dma_start(smp_d[4 * hf:4 * hf + 4].rearrange("b h s c -> (b h s) c"), so).then_inc(S("st_smp"), 16)
                    sp.wait_ge(S("st_smp"), 16 * (hf + 1))
                for q in range(2):
                    sp.wait_ge(S(f"st_att{q}"), 16 * 16)

            def rows_(step):
                sp.dma_start(wo, A["w_out"]).then_inc(S("ld_wo"), 16)
                sp.dma_start(rw, A["rw"]).then_inc(S("ld_wo"), 16)
                sp.dma_start(rb[0:1], A["rb"]).then_inc(S("ld_wo"), 16)
                sp.dma_start(nrow, A["nffn"].broadcast_to([P, D])).then_inc(S("ld_rows"), 16)
                for q, c in enumerate((2, 4, 3)):
                    sp.dma_start(grow[0][:, q], mod_d[0:1, c * D:(c + 1) * D].broadcast_to([P, D])).then_inc(S("ld_rows"), 16)
                    for b in range(NB):
                        sp.dma_start(grow[1][8 * b:8 * b + 8, q],
                                     mod_d[1 + b:2 + b, c * D:(c + 1) * D].broadcast_to([8, D])).then_inc(S("ld_rows"), 16)

            def mrg(i):
                r, t0 = rows(i), i * P
                if i >= 3:
                    sp.wait_ge(S("prj_mm"), 2 * (i - 2))
                sp.dma_start(mixl[:, i % 3, :, 0:r], mix_d[:, :, t0:t0 + r].rearrange("k p t -> p k t")).then_inc(S(f"ld_mix{i % 3}"), 16)
                if i >= 2:
                    sp.wait_ge(S("mrg_o"), i - 1)
                if i < NT - 1:
                    sp.dma_start(ma[:, i % 2].rearrange("p q h c -> p q (h c)"),
                                 att_d[:, t0:t0 + P].rearrange("q t c -> t q c")).then_inc(S(f"ld_ma{i % 2}"), 16)
                else:
                    for b in range(NB):
                        sp.dma_start(od[8 * b:8 * b + 8, i % 2].rearrange("p (h c) -> p h c", h=4),
                                     smp_d[b].rearrange("h s c -> s h c")).then_inc(S("ld_od"), 16)
                if i >= 2:
                    sp.wait_ge(S("x1_ready"), i - 1)
                sp.dma_start(xt[0:r, i % 2], A["x"][t0:t0 + r]).then_inc(S(f"ld_xt{i % 2}"), 16)

            def nrm(i):
                r, t0 = rows(i), i * P
                sp.wait_ge(S("h2_ready"), i + 1)
                sp.dma_start(x1_d[t0:t0 + r], x1[0:r, i % 2]).then_inc(S(f"st_x1{i % 2}"), 16)
                sp.dma_start(h2_d[t0:t0 + r], h2[0:r, i % 2]).then_inc(S(f"st_h2{i % 2}"), 16)

            def route(step):
                for q in range(2):
                    sp.wait_ge(S(f"st_x1{q}"), 16 * (9 - q))
                    sp.wait_ge(S(f"st_h2{q}"), 16 * (9 - q))
                sp.sem_inc(S("h2_stored"), 1)

            def moe(step):
                sp.wait_ge(S("route_done"), 1)
                parts = (("g_mm", wg, A["wg"]), ("u_mm", wu, A["wu"]), ("y_mm", wd, A["wd"]))

                def sub(it, q, u):
                    if q % 2:
                        return
                    b, s = it * 4 + q, q // 2
                    e = sp.value_load(bexp[0:1, bass.ds(it * 2 + s, 1)], min_val=0, max_val=NE - 1)

                    def work():
                        for name, w, src in parts:
                            if not isinstance(it, int) or it > 0:
                                sp.wait_ge(S(name), b - 2)
                            sp.dma_start(w[:, s].rearrange("p k n -> p (k n)"),
                                         src[bass.ds(e, 1)].rearrange("o p n -> (o p) n")).then_inc(S(f"ld_{name}{s}"), 16)
                    if_used(sp, u, work, [(f"ld_{name}{s}", it * 16, 16) for name, w, src in parts])
                quads(sp, sub, lambda it: [(f"ld_{name}{s}", it * 16, 16) for name, w, src in parts for s in range(2)])

            def comb(step):
                for q in range(NT):
                    r, t0 = rows(q), q * P
                    if q == 0:
                        sp.dma_start(g2r[:, 0], mod_d[0:1, 5 * D:6 * D].broadcast_to([P, D])).then_inc(S("ld_g2"), 16)
                        for b in range(NB):
                            sp.dma_start(g2r[8 * b:8 * b + 8, 1], mod_d[1 + b:2 + b, 5 * D:6 * D].broadcast_to([8, D])).then_inc(S("ld_g2"), 16)
                    if q >= 4:
                        sp.wait_ge(S(f"st_out{q % 4}"), 16 * (q // 4))
                    sp.dma_start(cx[0:r, q % 4], x1_d[t0:t0 + r]).then_inc(S(f"ld_cx{q % 4}"), 16)
                    if q >= 2:
                        store(q - 2)
                store(NT - 2)
                store(NT - 1)
                for q in range(4):
                    sp.wait_ge(S(f"st_out{q}"), 16 * len(range(q, NT, 4)))

            def store(q):
                r, t0 = rows(q), q * P
                sp.wait_ge(S("comb_done"), q + 1)
                sp.dma_start(O["y"][t0:t0 + r], cx[0:r, q % 4]).then_inc(S(f"st_out{q % 4}"), 16)

            run({"mod": mod, "norm1": norm1, "z": z, "qkv": qkv, "bar": bar, "tab": tab, "att": att, "smp": smp, "rows": rows_,
                 "row": parts((mrg, 0), (nrm, 2)), "route": route, "moe": moe, "comb": comb})

        @block.gpsimd
        def _(pool):
            link = linker(pool, "pool_own")
            link(pool.memset(zero, 0.0))
            pool.sem_inc(S("zero_ready"), 1)
            link(pool.memset(ones, 1.0))
            pool.sem_inc(S("ones_ready"), 1)

            def begin(step):
                if ORD[step]:
                    pool.wait_ge(S("mixer_done"), ORD[step])

            def ztile(sl, j):
                i = ZINDEX[(sl, j)]
                pool.wait_ge(S(f"z_stored{i % 2}"), 16 * (i // 2 + 1))
                return z_d[i]

            def lru(step, j):
                begin(step)
                xa = ztile(XA, j)
                pool.dma_start(buf[0][:, 3:3 + TP], xa[:, 0:TP]).then_inc(S("ld_lru"), 16)
                pool.dma_start(buf[0][:, 3 + TP:3 + TP + 88].rearrange("p (b s) -> p b s", b=NB)[:, :, 3:11],
                               xa[:, TP:T].rearrange("p (b s) -> p b s", b=NB)).then_inc(S("ld_lru"), 16)
                pool.dma_start(buf[6][:, 0:T], ztile(GA, j)).then_inc(S("ld_lru"), 16)
                pool.wait_ge(S("lru_h"), j + 1)
                hh, cc = buf[7 + j], buf[0]
                rows = slice(j * P, j * P + P)
                pool.dma_start(O["p_lru_h"][rows], buf[1][:, TP - 1:TP], allow_slow_non_contiguous=True).then_inc(S("st_mix"), 16)
                pool.dma_start(O["s_lru_h"][rows], sm[:, 16:24]).then_inc(S("st_mix"), 16)
                pool.dma_start(O["p_lru_conv"][rows], cc[:, TP:TP + 3]).then_inc(S("st_mix"), 16)
                pool.dma_start(O["s_lru_conv"][rows],
                               cc[:, 3 + TP:3 + TP + 88].rearrange("p (b s) -> p b s", b=NB)[:, :, 8:11]).then_inc(S("st_mix"), 16)

            def sconv(step, j):
                begin(step)
                pool.dma_start(buf[1][:, 0:T], ztile(GC, j)).then_inc(S("ld_sconv"), 16)
                pool.dma_start(buf[2][:, 0:T], ztile(XB, j)).then_inc(S("ld_sconv"), 16)
                pool.dma_start(buf[3][:, 0:T], ztile(GB, j)).then_inc(S("ld_sconv"), 16)
                pool.wait_ge(S("sconv_prod"), j + 1)
                rows = slice(j * P, j * P + P)
                pool.dma_start(O["p_sconv"][rows], buf[0][:, TP:TP + 2]).then_inc(S("st_mix"), 16)
                pool.dma_start(O["s_sconv"][rows],
                               buf[0][:, 2 + TP:2 + TP + 80].rearrange("p (b s) -> p b s", b=NB)[:, :, 8:10]).then_inc(S("st_mix"), 16)

            def s5prep(step, j):
                begin(step)
                link(pool.memset(toep, 0.0))
                pool.wait_ge(S("s5_kern"), j + 1)
                kern = buf[1][0:16, 0:GH * P].rearrange("p (g m) -> p g m", g=GH)
                for s in range(CL):
                    pool.dma_start(toep[16 * s:16 * s + 16, :, 16 * s:P], kern[:, :, 0:P - 16 * s]).then_inc(S("toep_ready"), 16)

            def s5(step, j):
                begin(step)
                u = ztile(UC, j).rearrange("(g c) (s n) -> s c g n", c=SC, s=CL)
                ub = buf[0][:, 0:GH * NC].rearrange("p (g n) -> p g n", g=GH)
                for s in range(CL):
                    pool.dma_start(ub[16 * s:16 * s + 16], u[s]).then_inc(S("ld_u"), 16)
                hb = buf[5][:, 0:GH * NC].rearrange("p (g n) -> p g n", g=GH)
                pool.dma_start(hb[:, :, NCP:NC], A["s5_0"][:, GH * j:GH * j + GH]).then_inc(S("ld_u"), 16)
                pool.wait_ge(S("s5_y"), j + 1)
                pool.wait_ge(S("s5_fin"), j + 1)
                yb = buf[7][:, 0:GH * NC].rearrange("p (g n) -> p g n", g=GH)
                yd = y5_d[j].rearrange("(g c) (s n) -> s c g n", c=SC, s=CL)
                for s in range(CL):
                    pool.dma_start(yd[s], yb[16 * s:16 * s + 16]).then_inc(S("st_y5"), 16)
                pool.dma_start(O["p_s5"][:, GH * j:GH * j + GH], hfin_p[:, GH * j:GH * j + GH]).then_inc(S("st_mix"), 16)
                pool.dma_start(O["s_s5"][:, GH * j:GH * j + GH], hfin_s[:, GH * j:GH * j + GH]).then_inc(S("st_mix"), 16)

            def glu(step):
                begin(step)
                pool.dma_start(buf[6][:, 0:1024], A["glu_w"]).then_inc(S("ld_glu"), 16)
                pool.wait_ge(S("st_y5"), 16 * 2 * CL)
                for j in range(2):
                    pool.dma_start(buf[j][:, 0:T], y5_d[j]).then_inc(S("ld_glu"), 16)
                    pool.dma_start(buf[2 + j][:, 0:T], ztile(UC, j)).then_inc(S("ld_glu"), 16)

            def out(step):
                row = {"outA": 0, "outB": 2, "outC": 4}[step[0]]
                pool.wait_ge(S("out_normed"), OUTN[step[0]])
                for j in range(2):
                    pool.dma_start(mix_d[row + j], buf[3 + j][:, 0:T]).then_inc(S("st_mixd"), 16)

            def bar(step, n):
                if n == 1:
                    pool.wait_ge(S("st_mix"), 16 * 16)
                    pool.wait_ge(S("st_mixd"), 16 * 6)
                barrier(pool)(step, n)

            def route(step):
                link(pool.memset(zero_i, 0))
                link(pool.iota(tids, pattern=[[P, NT]], base=0, channel_multiplier=1))
                link(pool.iota(io_i, pattern=[[1, 32]], base=-64, channel_multiplier=0))
                link(pool.iota(blk_i, pattern=[[P, NSUB]], base=0, channel_multiplier=0))
                link(pool.memset(tri, 1.0))
                link(pool.affine_select(out=tri, in_=tri, compare_op=ALU.is_gt, fill=0.0, base=0, pattern=[[1, P]], channel_multiplier=-1))
                pool.dma_start(tok_d.rearrange("(p b) o -> p (b o)", p=P), zero_i).then_inc(S("st_zero"), 16)
                pool.sem_inc(S("route_const"), 1)
                pool.wait_ge(S("st_zero"), 16)
                pool.wait_ge(S("dest_ready"), 1)
                for i in range(NT):
                    r = rows(i)
                    for k in range(2):
                        pool.indirect_dma_start(out=tok_d, out_offset=bass.IndirectOffsetOnAxis(ap=dest[0:r, i, k:k + 1], axis=0),
                                                in_=tids[0:r, i:i + 1], in_offset=None).then_inc(S("st_tok"), 16)
                pool.wait_ge(S("st_tok"), 16 * 2 * NT)
                pool.dma_start(toks, tok_d.rearrange("(b p) o -> p (b o)", p=P), allow_slow_non_contiguous=True).then_inc(S("ld_toks"), 16)
                pool.wait_ge(S("ld_toks"), 16)
                pool.wait_ge(S("h2_stored"), 1)
                pool.wait_ge(S("route_done"), 1)

            def moe(step):
                def sub(it, q, u):
                    b, s = it * 4 + q, q % 2
                    if not (isinstance(b, int) and b < 2):
                        pool.wait_ge(S("xT_mm"), 2 * b - 2)
                        pool.sem_inc(S("xg_turn"), 1)
                        pool.wait_ge(S(f"ld_xg{s}"), it * 32 + 16 * (q // 2))
                    pool.tensor_copy(tokc[:, s:s + 1], toks[:, bass.ds(b, 1)]).then_inc(S("tok_copied"), 1)
                    pool.wait_ge(S("tok_copied"), b + 1)
                    pool.sem_inc(S("xg_turn"), 1)
                    pool.indirect_dma_start(out=xg[:, s], out_offset=None, in_=h2_d,
                                            in_offset=bass.IndirectOffsetOnAxis(ap=tokc[:, s:s + 1], axis=0)).then_inc(S(f"ld_xg{s}"), 16)
                    if q == 3:
                        for n in range(2):
                            pool.wait_ge(S(f"ld_xg{n}"), it * 32 + 32)
                quads(pool, sub, lambda it: [("tok_copied", it * 4, 4)])

            def comb(step):
                for q in range(NT):
                    r = rows(q)
                    if q >= 4:
                        pool.wait_ge(S("comb_done"), q - 3)
                    for k in range(2):
                        pool.indirect_dma_start(out=cy[0:r, q % 4, k], out_offset=None, in_=ye_d,
                                                in_offset=bass.IndirectOffsetOnAxis(ap=dest[0:r, q, k:k + 1], axis=0)).then_inc(S(f"ld_cy{q % 4}"), 16)

            run({"A": lru, "B": sconv, "s5prep": s5prep, "s5": s5, "glu": glu, "outA": out, "outB": out, "outC": out,
                 "bar": bar, "route": route, "moe": moe, "comb": comb})

        @block.scalar
        def _(act):
            link = linker(act, "act_own")

            def mod(step):
                act.wait_ge(S("ld_vec"), 16 * 5)
                link(act.activation(cS, cT, ACT.Silu))
                act.sem_inc(S("c_silu"), 1)

            def mod_rows():
                for n in range(12):
                    act.wait_ge(S("mod_mm"), n + 1)
                    link(act.copy(modrow[0:9, n * 512:(n + 1) * 512], bank[n % 2][0:9, :]))
                    act.sem_inc(S("mod_row"), 1)
                act.dma_start(mod_d, modrow[0:9, :]).then_inc(S("mod_stored"), 16)

            def s5par(step):
                act.wait_ge(S("ld_s5"), 32)
                link(act.activation(s5p[:, 3], s5p[:, 2], ACT.Exp))
                act.sem_inc(S("s5_step"), 1)
                act.wait_ge(S("s5_ang"), 1)
                link(act.activation(s5p[:, 6], s5p[:, 4], ACT.Exp))
                link(act.activation(s5p[:, 13], s5p[:, 4], ACT.Exp, scale=float(CL)))
                link(act.activation(s5p[:, 8], s5p[:, 14], ACT.Sin))
                link(act.activation(s5p[:, 7], s5p[:, 15], ACT.Sin))
                link(act.activation(sm[:, 4:6], sm[:, 2:4], ACT.Exp))
                act.sem_inc(S("s5_trig"), 1)
                mod_rows()

            def norm1(step):
                act.wait_ge(S("mod_stored"), 16)
                act.wait_ge(S("modT_ready"), 1)
                for c, (t0, w) in enumerate(CHUNKS):
                    act.wait_ge(S(f"ld_x{c}"), 16)
                    for k in range(KT):
                        n = c * KT + k
                        if n >= 2:
                            act.wait_ge(S("norm1_mm"), n - 1)
                        link(act.activation(sq1[:, n % 2, 0:w], hT[:, k, t0:t0 + w], ACT.Square))
                        act.sem_inc(S("norm1_sq"), 1)
                    act.wait_ge(S("norm1_var"), c + 1)
                    link(act.activation(rst1[:, 0:w], rst1[:, 0:w], ACT.Sqrt))
                    act.sem_inc(S("norm1_sqrt"), 1)
                    act.wait_ge(S("norm1_x"), c + 1)
                    if c < 4:
                        for k in range(KT):
                            link(act.activation(hT[:, k, t0:t0 + w], hT[:, k, t0:t0 + w], ACT.Identity,
                                                bias=modT[:, k, 0:1], scale=sc1[:, k, 0:1]))
                        act.sem_inc(S("h_ready"), 1)

            def z(step, i):
                sl, j = ZTILES[i]
                if i >= 2:
                    act.wait_ge(S(f"z_stored{i % 2}"), 16 * (i // 2))
                for c, (t0, w) in enumerate(CHUNKS):
                    n = 5 * i + c
                    act.wait_ge(S("z_mm"), n + 1)
                    if sl == UC:
                        o = zst[:, i % 2].rearrange("p (s n) -> p n s", s=CL)[:, t0 // CL:(t0 + w) // CL, :]
                        link(act.copy(o, bank[n % 2][:, 0:w].rearrange("p (n s) -> p n s", s=CL)))
                    else:
                        link(act.copy(zst[:, i % 2, t0:t0 + w], bank[n % 2][:, 0:w]))
                    act.sem_inc(S("z_free"), 1)
                act.dma_start(z_d[i], zst[:, i % 2]).then_inc(S(f"z_stored{i % 2}"), 16)

            def lru(step, j):
                act.wait_ge(S("lru_par"), 1)
                for q, (dst, b) in enumerate(((buf[2], "ba"), (buf[3], "bx"))):
                    for c, (t0, w) in enumerate(CHUNKS):
                        n = base[step] + 5 * q + c
                        act.wait_ge(S("mx_full"), n + 1)
                        link(act.activation(dst[:, t0:t0 + w], mx(n)[:, 0:w], ACT.Sigmoid, bias=V(b, j)))
                        act.sem_inc(S(f"mx_free{n % RB}"), 1)
                link(act.activation(buf[2][:, 0:T], buf[2][:, 0:T], ACT.Tanh, scale=sm[:, 8 + j:9 + j]))
                link(act.activation(buf[4][:, 0:T], buf[2][:, 0:T], ACT.Sqrt, scale=-1.0))
                act.sem_inc(S("lru_w"), 1)
                act.wait_ge(S("ld_lru"), 48 * (j + 1))
                link(act.activation(buf[6][:, 0:T], buf[6][:, 0:T], ACT.Gelu_apprx_tanh))
                act.sem_inc(S("lru_g"), 1)

            def s5(step, j):
                b0 = base[step] + 21
                for g in range(GH):
                    act.wait_ge(S("mx_full"), b0 + g + 1)
                    link(act.copy(buf[7][:, g * NC:(g + 1) * NC], mx(b0 + g)[:, 0:NC]))
                    act.sem_inc(S(f"mx_free{(b0 + g) % RB}"), 1)
                act.sem_inc(S("s5_y"), 1)

            def glu(step):
                act.wait_ge(S("glu_y"), 1)
                for j in range(2):
                    link(act.activation(buf[4 + j][:, 0:T], buf[j][:, 0:T], ACT.Gelu_apprx_tanh))
                act.sem_inc(S("glu_gelu"), 1)
                for m in range(4):
                    for c, (t0, w) in enumerate(CHUNKS):
                        n = base[step] + 5 * m + c
                        act.wait_ge(S("mx_full"), n + 1)
                        link(act.activation(buf[m][:, t0:t0 + w], mx(n)[:, 0:w],
                                            ACT.Identity if m < 2 else ACT.Sigmoid, bias=V("glu_b", m)))
                        act.sem_inc(S(f"mx_free{n % RB}"), 1)
                act.sem_inc(S("glu_done"), 1)

            def out(step):
                act.wait_ge(S("mixer_done"), ORD[step])
                for j in range(2):
                    link(act.activation(buf[j][:, 0:T], buf[7 + j][:, 0:T], ACT.Square))
                act.sem_inc(S("out_sq"), 1)
                act.wait_ge(S("out_var"), OUTN[step[0]])
                link(act.activation(buf[2][:, 0:T], buf[2][:, 0:T], ACT.Sqrt))
                act.sem_inc(S("out_sqrt"), 1)

            def qkv(step, i):
                if i < NT:
                    r, t0 = rows(i), i * P
                    act.wait_ge(S("v_mm"), i + 1)
                    if i >= 2:
                        act.wait_ge(S(f"st_v{i % 2}"), 16 * (i // 2))
                    link(act.copy(vst[0:r, i % 2], bank[7][0:r, 0:256]))
                    act.sem_inc(S("v_free"), 1)
                    act.dma_start(O["v"][t0:t0 + r], vst[0:r, i % 2]).then_inc(S(f"st_v{i % 2}"), 16)
                    if i:
                        act.wait_ge(S("qk_ss"), i)
                    link(act.activation(ksq[0:r], bank[i % 2][0:r], ACT.Square))
                    act.sem_inc(S("qk_sq"), 1)
                    act.wait_ge(S("qk_ss"), i + 1)
                    link(act.activation(kss[0:r], kss[0:r], ACT.Sqrt))
                    act.sem_inc(S("qk_sqrt"), 1)
                if i:
                    n = base[step]
                    r = rows(i - 1)
                    act.wait_ge(S("mx_full"), n + 1)
                    if i >= 2:
                        act.wait_ge(S("st_qkT"), 16 * (i - 1))
                    link(act.copy(tst[:, :, 0:r], mx(n).rearrange("p (n t) -> p n t", n=4)[:, :, 0:r]))
                    act.sem_inc(S(f"mx_free{n % RB}"), 1)
                    act.sem_inc(S("qkT_ready"), 1)

            def bar(step, n):
                if n == 1:
                    for q in range(2):
                        act.wait_ge(S(f"st_v{q}"), 16 * (9 - q))
                if n == 4:
                    for q in range(2):
                        act.wait_ge(S(f"st_ye{q}"), 16 * NSUB // 2)
                barrier(act)(step, n)

            def tab(step):
                for c in range(7):
                    w = min(512, L1 + L2 + L3 - 512 * c)
                    act.wait_ge(S("tab_mm"), c + 1)
                    link(act.copy(tabs[0:4, 512 * c:512 * c + w], bank[c][0:4, 0:w]))
                act.sem_inc(S("tab_done"), 1)

            def att(step):
                def exps(u):
                    w = 128 * len(BLOCKS[u // 4][4])
                    act.wait_ge(S("att_max"), u + 1)
                    if u >= 4:
                        act.wait_ge(S("att_pT"), u - 3)
                    link(act.activation(pp[:, u % 4, 0:w], ssb[:, u % 4, 0:w], ACT.Exp, bias=nmax[:, u % 4:u % 4 + 1],
                                        accum_out=ost[:, (u // 4) % 2, u % 4, 65:66]))
                    act.sem_inc(S("att_exp"), 1)

                def evac(u):
                    if u % 2:
                        w = 128 * len(BLOCKS[u // 4][4])
                        act.wait_ge(S("att_pT"), u + 1)
                        if u >= 4:
                            act.wait_ge(S("att_pv"), u - 3)
                        link(act.copy(pt[:, u % 4, 0:w], bank[2 + u % 2][:, 0:w]))
                        act.sem_inc(S("att_ptA"), 1)
                for u in range(NU + 1):
                    if u < NU:
                        exps(u)
                    if u >= 1:
                        evac(u - 1)

            def smp(step):
                for hf in range(2):
                    act.wait_ge(S("smp_max"), hf + 1)
                    link(act.activation(spp, sss, ACT.Exp, bias=sst[:, 1:2], accum_out=sst[:, 2:3]))
                    act.sem_inc(S("smp_exp"), 1)
                    for q in range(3):
                        act.wait_ge(S("smp_pT"), 3 * hf + q + 1)
                        w = 4 if q < 2 else 2
                        link(act.copy(spt[:, 4 * q:4 * q + w], bank[3 + q][:, 0:P * w].rearrange("p (n m) -> p n m", m=P)))
                        if q == 2:
                            link(act.copy(spt[0:8, 10], bank[5][0:8, 2 * P:3 * P]))
                        act.sem_inc(S("smp_pt"), 1)

            def mrg(i):
                r = rows(i)
                if i < NT - 1:
                    act.wait_ge(S("mrg_d"), i + 1)
                    link(act.activation(mw[:, 4:6], mw[:, 2:4], ACT.Exp))
                    act.sem_inc(S("mrg_e"), 1)
                act.wait_ge(S("mrg_ss"), i + 1)
                link(act.activation(mw[0:r, 9, 0:1], mw[0:r, 9, 0:1], ACT.Sqrt))
                act.sem_inc(S("mrg_sqrt"), 1)
                act.wait_ge(S("odT_mm"), i + 1)
                if i >= 2:
                    act.wait_ge(S("prj_mm"), 2 * (i - 1))
                for k in range(2):
                    link(act.activation(odt[:, i % 2, k, 0:r], bank[4][:, k * P:k * P + r], ACT.Copy, scale=V("out_norm", 6 + k)))
                act.sem_inc(S("odT_ready"), 1)

            def nrm(i):
                r = rows(i)
                act.wait_ge(S("x1_ready"), i + 1)
                link(act.activation(xsq[0:r], x1[0:r, i % 2], ACT.Square, accum_out=mw[0:r, 10, 0:1]))
                act.sem_inc(S("x1_ss"), 1)
                act.wait_ge(S("x1_var"), i + 1)
                link(act.activation(mw[0:r, 10, 0:1], mw[0:r, 10, 0:1], ACT.Sqrt))
                act.sem_inc(S("x1_sqrt"), 1)

            def logits(i):
                r = rows(i)
                act.wait_ge(S("lg_mm"), i + 1)
                link(act.copy(lg[0:r, i], bank[5][0:r, 0:36]))
                act.sem_inc(S("lg_free"), 1)

            def turned(i):
                r = rows(i)
                for q in range(2):
                    act.wait_ge(S("h2T_mm"), 2 * i + q + 1)
                    link(act.copy(h2T[:, i % 2, 4 * q:4 * q + 4, 0:r],
                                  bank[2 + q][:, :].rearrange("p (k t) -> p k t", k=4)[:, :, 0:r]))
                act.sem_inc(S("h2T_ready"), 1)

            def route(step):
                act.wait_ge(S("rt_x"), 1)
                link(act.activation(rs[:, 0, :, 0:4], rs[:, 0, :, 0:4], ACT.Exp))
                link(act.activation(rs[:, 1, :, 0], rs[:, 1, :, 0], ACT.Exp))
                act.sem_inc(S("rt_e"), 1)

            def moe(step):
                act.wait_ge(S("route_done"), 1)

                def xt_half(b, s, u):
                    def work():
                        act.wait_ge(S("xT_mm"), b * 2 + 2)
                        act.copy(xgT[:, s, 4:8], bank[1][:, :].rearrange("p (k t) -> p k t", k=4)).then_inc(S("xtA"), 1)
                    if_used(act, u, work, [("xtA", b, 1)])

                def silu(b, u):
                    def work():
                        act.wait_ge(S("g_mm"), b + 1)
                        if not (isinstance(b, int) and b == 0):
                            act.wait_ge(S("h_ready2"), b)
                        act.activation(gs, bank[2][:, :], ACT.Silu).then_inc(S("silu"), 1)
                    if_used(act, u, work, [("silu", b, 1)])

                def sub(it, q, u):
                    b, s = it * 4 + q, q % 2
                    first = isinstance(b, int) and b < 2
                    stored = it * 32 + 16 * (q // 2)
                    last = isinstance(it, int) and it == LAST
                    if not (last and q == 3):
                        silu(b + 1, flag(act, b + 1))
                    if not (last and q >= 2):
                        xt_half(b + 2, s, flag(act, b + 2))

                    def work():
                        act.wait_ge(S("y_mm"), b + 1)
                        if not first:
                            act.wait_ge(S(f"st_ye{s}"), stored)
                        act.copy(yb[:, s, 512:1024], bank[5][:, :]).then_inc(S("yA"), 1)
                        act.wait_ge(S("yA"), b + 1)
                        act.wait_ge(S("yV"), b + 1)
                        act.dma_start(ye_d[bass.ds(b * P, P)], yb[:, s]).then_inc(S(f"st_ye{s}"), 16)
                    if_used(act, u, work, [("yA", b, 1), (f"st_ye{s}", stored, 16)])
                xt_half(0, 0, None)
                silu(0, None)
                xt_half(1, 1, flag(act, 1))
                quads(act, sub, lambda it: [("silu", it * 4 + 1, 4), ("xtA", it * 4 + 2, 4), ("yA", it * 4, 4),
                                            ("st_ye0", it * 32, 32), ("st_ye1", it * 32, 32)])

            run({"mod": mod, "s5par": s5par, "norm1": norm1, "z": z, "A": lru, "s5": s5, "glu": glu,
                 "outA": out, "outB": out, "outC": out, "qkv": qkv, "bar": bar, "tab": tab, "att": att, "smp": smp,
                 "row": parts((nrm, 2), (mrg, 0), (logits, 3), (turned, 2)), "route": route, "moe": moe})

        @block.vector
        def _(dve):
            link = linker(dve, "dve_own")
            TT, STT, TS = dve.tensor_tensor, dve.scalar_tensor_tensor, dve.tensor_scalar

            def bc(ap, w):
                return ap.unsqueeze(2).broadcast_to([ap.shape[0], ap.shape[1], w])

            def s5par(step):
                ar, ai, ldt, stp, ex, ang, mag, co, si, abr, abi, zr, zi, m8, t1, t2 = (s5p[:, n] for n in range(16))
                BX, BY, CX, CY = (s5b[:, n] for n in range(4))
                dve.wait_ge(S("ld_vec"), 16 * 5)
                dve.wait_ge(S("ld_s5"), 32)
                dve.wait_ge(S("s5_step"), 1)
                link(TT(ex, ar, stp, ALU.mult))
                link(TT(ang, ai, stp, ALU.mult))

                def reduce_angle(dst, shift):
                    link(TS(dst, ang, shift, None, ALU.add))
                    link(TS(mag, dst, float(0.5 / np.pi), 12582912.0, ALU.mult, ALU.add))
                    link(TS(mag, mag, 12582912.0, None, ALU.subtract))
                    link(STT(dst, mag, -6.28125, dst, ALU.mult, ALU.add))
                    link(STT(dst, mag, float(-(2 * np.pi - 6.28125)), dst, ALU.mult, ALU.add))
                    link(TS(dst, dst, 3.1415925, -3.1415925, ALU.min, ALU.max))
                reduce_angle(t1, 0.0)
                reduce_angle(t2, float(np.pi / 2))
                lam = V("lam")
                link(TS(sm[:, 0:2], lam, -1.0, None, ALU.mult))
                link(TT(sm[:, 2:4], sm[:, 0:2], lam, ALU.min))
                dve.sem_inc(S("s5_ang"), 1)
                dve.wait_ge(S("s5_trig"), 1)
                y = sm[:, 4:6]
                link(TS(sm[:, 6:8], y, 2.0, None, ALU.add))
                link(dve.reciprocal(sm[:, 6:8], sm[:, 6:8]))
                link(TT(sm[:, 6:8], sm[:, 6:8], y, ALU.mult))
                link(TT(sm[:, 10:12], sm[:, 6:8], sm[:, 6:8], ALU.mult))
                link(TS(sm[:, 12:14], sm[:, 10:12], 0.0, 1.0 / 17, ALU.mult, ALU.add))
                for q in (15, 13, 11, 9, 7, 5, 3, 1):
                    link(TT(sm[:, 12:14], sm[:, 12:14], sm[:, 10:12], ALU.mult))
                    link(TS(sm[:, 12:14], sm[:, 12:14], 1.0 / q, None, ALU.add))
                link(TT(sm[:, 12:14], sm[:, 12:14], sm[:, 6:8], ALU.mult))
                link(TS(sm[:, 12:14], sm[:, 12:14], 2.0, None, ALU.mult))
                link(STT(sm[:, 12:14], sm[:, 0:2], 0.0, sm[:, 12:14], ALU.max, ALU.add))
                link(TS(sm[:, 8:10], sm[:, 12:14], -4.0, None, ALU.mult))
                dve.sem_inc(S("lru_par"), 1)
                link(TT(abr, mag, co, ALU.mult))
                link(TT(abi, mag, si, ALU.mult))
                link(TT(t1, ar, ar, ALU.mult))
                link(TT(t2, ai, ai, ALU.mult))
                link(TT(t1, t1, t2, ALU.add))
                link(dve.reciprocal(t1, t1))
                link(STT(zr, abr, 1.0, ar, ALU.subtract, ALU.mult))
                link(TT(t2, abi, ai, ALU.mult))
                link(TT(zr, zr, t2, ALU.add))
                link(TT(zr, zr, t1, ALU.mult))
                link(STT(zi, abr, 1.0, ai, ALU.subtract, ALU.mult))
                link(TT(t2, abi, ar, ALU.mult))
                link(TT(zi, t2, zi, ALU.subtract))
                link(TT(zi, zi, t1, ALU.mult))
                link(TS(BY, BY, V("sgn"), None, ALU.mult))
                link(TS(CX, CX, V("sgn"), -1.0, ALU.mult, ALU.mult))
                link(TS(CY, CY, -1.0, None, ALU.mult))
                xt = ff.rearrange("p g d c -> p (g d c)")
                p1, p2, p3, p4 = (xt[:, 256 * q:256 * q + 256].rearrange("p (g c) -> p g c", g=G16) for q in range(4))
                link(TT(p1, BX, bc(zr, SC), ALU.mult))
                link(TT(p2, BY, bc(zi, SC), ALU.mult))
                link(TT(p3, BY, bc(zr, SC), ALU.mult))
                link(TT(p4, BX, bc(zi, SC), ALU.mult))
                link(TT(BX, p1, p2, ALU.add))
                link(TT(BY, p3, p4, ALU.subtract))

                def cmul(orr, oi, xr, xi, yr, yi):
                    link(TT(t1, xr, yr, ALU.mult))
                    link(TT(t2, xi, yi, ALU.mult))
                    link(TT(ldt, xr, yi, ALU.mult))
                    link(TT(oi, xi, yr, ALU.mult))
                    link(TT(oi, oi, ldt, ALU.add))
                    link(TT(orr, t1, t2, ALU.subtract))
                link(dve.memset(pwr[:, 0], 1.0))
                link(dve.memset(pwi[:, 0], 0.0))
                for d in range(1, CL + 1):
                    cmul(pwr[:, d], pwi[:, d], pwr[:, d - 1], pwi[:, d - 1], abr, abi)
                link(dve.tensor_copy(rot[:, 0, 8], co))
                link(dve.tensor_copy(rot[:, 1, 8], si))
                for _ in range(2):
                    cmul(stp, ang, rot[:, 0, 8], rot[:, 1, 8], rot[:, 0, 8], rot[:, 1, 8])
                    link(dve.tensor_copy(rot[:, 0, 8], stp))
                    link(dve.tensor_copy(rot[:, 1, 8], ang))
                cmul(rot[:, 0, 0], rot[:, 1, 0], rot[:, 0, 8], rot[:, 1, 8], rot[:, 0, 8], rot[:, 1, 8])
                for lv in range(1, 8):
                    cmul(rot[:, 0, lv], rot[:, 1, lv], rot[:, 0, lv - 1], rot[:, 1, lv - 1], rot[:, 0, lv - 1], rot[:, 1, lv - 1])
                dve.wait_ge(S("modT_mm"), 1)
                link(dve.tensor_copy(modT, bank[2][:, 0:144].rearrange("p (k b) -> p k b", b=9)))
                link(STT(sc1, modT[:, 8:16, :], 1.0, bc(V("norm_mix"), 9), ALU.add, ALU.mult))
                dve.sem_inc(S("modT_ready"), 1)

            def norm1(step):
                dve.wait_ge(S("mod_stored"), 16)
                for c, (t0, w) in enumerate(CHUNKS):
                    dve.wait_ge(S("norm1_mm"), KT * (c + 1))
                    link(TS(rst1[:, 0:w], bank[0][:, 0:w], 1.0 / D, EPS, ALU.mult, ALU.add))
                    dve.sem_inc(S("norm1_var"), 1)
                    dve.wait_ge(S("norm1_sqrt"), c + 1)
                    link(dve.reciprocal(rst1[:, 0:w], rst1[:, 0:w]))
                    x = hT[:, :, t0:t0 + w]
                    link(TT(x, x, rst1[:, 0:w].unsqueeze(1).broadcast_to([P, KT, w]), ALU.mult))
                    dve.sem_inc(S("norm1_x"), 1)
                    if c == 4:
                        for k in range(KT):
                            xs = hT[:, k, TP:T].rearrange("p (b s) -> p b s", b=NB)
                            link(TT(xs, xs, bc(sc1[:, k, 1:9], NS), ALU.mult))
                            link(TT(xs, xs, bc(modT[:, k, 1:9], NS), ALU.add))
                        dve.sem_inc(S("hs_ready"), 1)

            def lru(step, j):
                xp, xs = buf[0], buf[0][:, 3 + TP:3 + TP + 88].rearrange("p (b s) -> p b s", b=NB)
                y, w, ig, sq, a, t = (buf[q][:, 0:T] for q in (1, 2, 3, 4, 5, 7 + j))
                d = buf[7 + j][:, 0:T]
                link(dve.memset(xp[:, 0:3], 0.0))
                link(dve.tensor_copy(xs[:, :, 0:3], V("conv0")[:, 24 * j:24 * j + 24].rearrange("p (b s) -> p b s", b=NB)))
                dve.wait_ge(S("ld_lru"), 48 * (j + 1))
                cw = [V("conv_w", 4 * j + q) for q in range(4)]
                ys = y[:, TP:T].rearrange("p (b s) -> p b s", b=NB)
                link(TS(y[:, 0:TP], xp[:, 0:TP], cw[0], V("conv_b", j), ALU.mult, ALU.add))
                link(TS(ys, xs[:, :, 0:8], cw[0], V("conv_b", j), ALU.mult, ALU.add))
                for q in range(1, 4):
                    link(STT(y[:, 0:TP], xp[:, q:q + TP], cw[q], y[:, 0:TP], ALU.mult, ALU.add))
                    link(STT(ys, xs[:, :, q:q + 8], cw[q], ys, ALU.mult, ALU.add))
                dve.sem_inc(S("lru_y"), 1)
                dve.wait_ge(S("lru_w"), j + 1)
                link(TS(d, w, -1.0, 1.0, ALU.mult, ALU.add))
                link(dve.reciprocal(d, d))
                link(STT(a, w, 1.0, d, ALU.add, ALU.mult))
                link(STT(sq, sq, 2.0, d, ALU.mult, ALU.mult))
                link(TT(sq, sq, ig, ALU.mult))
                link(TT(sq, sq, y, ALU.mult))
                a0 = a[:, TP:T].rearrange("p (b s) -> p b s", b=NB)[:, :, 0]
                b0 = sq[:, TP:T].rearrange("p (b s) -> p b s", b=NB)[:, :, 0]
                link(TT(sm[:, 24:32], a0, V("h0")[:, 8 * j:8 * j + 8], ALU.mult))
                link(TT(b0, b0, sm[:, 24:32], ALU.add))
                link(dve.memset(a0, 0.0))
                link(dve.tensor_tensor_scan(y, a, sq, 0.0, ALU.mult, ALU.add))
                link(dve.tensor_copy(sm[:, 16:24], y[:, TP:T].rearrange("p (b s) -> p b s", b=NB)[:, :, 7]))
                dve.sem_inc(S("lru_h"), 1)
                dve.wait_ge(S("lru_g"), j + 1)
                link(TT(buf[7 + j][:, 0:T], y, buf[6][:, 0:T], ALU.mult))
                dve.wait_ge(S("st_mix"), ST_MIX[step])
                dve.sem_inc(S("mixer_done"), 1)

            def sconv(step, j):
                pp, ps = buf[0], buf[0][:, 2 + TP:2 + TP + 80].rearrange("p (b s) -> p b s", b=NB)
                link(dve.memset(pp[:, 0:2], 0.0))
                link(dve.tensor_copy(ps[:, :, 0:2], V("sconv0")[:, 16 * j:16 * j + 16].rearrange("p (b s) -> p b s", b=NB)))
                dve.wait_ge(S("ld_sconv"), 48 * (j + 1))
                gc, xb, gb, y = (buf[q][:, 0:T] for q in (1, 2, 3, 4))
                vs = [v[:, TP:T].rearrange("p (b s) -> p b s", b=NB) for v in (gc, xb, gb, y)]
                link(TT(pp[:, 2:2 + TP], gc[:, 0:TP], xb[:, 0:TP], ALU.mult))
                link(TT(ps[:, :, 2:10], vs[0], vs[1], ALU.mult))
                dve.sem_inc(S("sconv_prod"), 1)
                for q in range(3):
                    cw = V("sconv_w", 3 * j + q)
                    if q == 0:
                        link(TS(y[:, 0:TP], pp[:, 0:TP], cw, None, ALU.mult))
                        link(TS(vs[3], ps[:, :, 0:8], cw, None, ALU.mult))
                    else:
                        link(STT(y[:, 0:TP], pp[:, q:q + TP], cw, y[:, 0:TP], ALU.mult, ALU.add))
                        link(STT(vs[3], ps[:, :, q:q + 8], cw, vs[3], ALU.mult, ALU.add))
                link(TT(buf[7 + j][:, 0:T], gb, y, ALU.mult))
                dve.wait_ge(S("st_mix"), ST_MIX[step])
                dve.sem_inc(S("mixer_done"), 1)

            def s5prep(step, j):
                X, Y, CX, CY = (s5b[:, n, GH * j:GH * j + GH] for n in range(4))
                gs = slice(GH * j, GH * j + GH)
                t1 = buf[2][:, 0:128].rearrange("p (g c) -> p g c", g=GH)
                t2 = buf[2][:, 128:256].rearrange("p (g c) -> p g c", g=GH)
                for d in range(CL + 1):
                    link(TT(t1, CX, bc(pwr[:, d, gs], SC), ALU.mult))
                    link(TT(t2, CY, bc(pwi[:, d, gs], SC), ALU.mult))
                    link(TT(ff[:, :, d, :], t1, t2, ALU.add))
                dve.sem_inc(S("s5_ff"), 1)
                et = buf[0][:, 0:1024].rearrange("p (g s c) -> p g s c", g=GH, s=CL)
                for s in range(CL):
                    link(TT(t1, X, bc(pwr[:, CL - 1 - s, gs], SC), ALU.mult))
                    link(TT(t2, Y, bc(pwi[:, CL - 1 - s, gs], SC), ALU.mult))
                    link(TT(et[:, :, s, :], t1, t2, ALU.add))
                dve.sem_inc(S("s5_et"), 1)
                b0 = base[step]
                for q in range(2):
                    dve.wait_ge(S("mx_full"), b0 + q + 1)
                    link(dve.tensor_copy(buf[1][0:16, 512 * q:512 * q + 512], mx(b0 + q)[0:16, :]))
                    dve.sem_inc(S(f"mx_free{(b0 + q) % RB}"), 1)
                dve.sem_inc(S("s5_kern"), 1)
                for q in range(2):
                    dve.wait_ge(S("mx_full"), b0 + q + 3)
                    m = mx(b0 + 2 + q)[:, :].rearrange("p (g m) -> p g m", g=4)
                    link(dve.tensor_copy(emat[:, 4 * q:4 * q + 4, :], m))
                    link(TS(emat2[:, 4 * q:4 * q + 4, 0:64], m[:, :, 64:128], -1.0, None, ALU.mult))
                    link(dve.tensor_copy(emat2[:, 4 * q:4 * q + 4, 64:128], m[:, :, 0:64]))
                    dve.sem_inc(S(f"mx_free{(b0 + 2 + q) % RB}"), 1)
                dve.wait_ge(S("toep_ready"), 16 * CL * (j + 1))
                dve.sem_inc(S("mixer_done"), 1)

            def s5(step, j):
                gs = slice(GH * j, GH * j + GH)
                ct, st, gi, gg, tmp = (buf[q][:, 0:GH * NCP].rearrange("p (g n) -> p g n", g=GH) for q in (1, 2, 3, 4, 6))
                hb = buf[5][:, 0:GH * NC].rearrange("p (g n) -> p g n", g=GH)
                link(dve.memset(ct[:, :, 0:1], 1.0))
                link(dve.memset(st[:, :, 0:1], 0.0))
                for lv in range(8):
                    L = 1 << lv
                    cr, ci = bc(rot[:, 0, lv, gs], L), bc(rot[:, 1, lv, gs], L)
                    link(TT(gi[:, :, 0:L], ct[:, :, 0:L], cr, ALU.mult))
                    link(TT(gg[:, :, 0:L], st[:, :, 0:L], ci, ALU.mult))
                    link(TT(ct[:, :, L:2 * L], gi[:, :, 0:L], gg[:, :, 0:L], ALU.subtract))
                    link(TT(gi[:, :, 0:L], ct[:, :, 0:L], ci, ALU.mult))
                    link(TT(gg[:, :, 0:L], st[:, :, 0:L], cr, ALU.mult))
                    link(TT(st[:, :, L:2 * L], gi[:, :, 0:L], gg[:, :, 0:L], ALU.add))
                ssm = hfin[:, 144:208].rearrange("p (g b) -> p g b", g=GH)
                b0 = base[step]
                for g in range(GH):
                    n = b0 + 2 * g
                    dve.wait_ge(S("mx_full"), n + 1)
                    link(TT(gi[:, g], mx(n)[:, 0:NCP], ct[:, g], ALU.mult))
                    link(dve.tensor_copy(ssm[:, g], mx(n)[:, NCP:NC]))
                    dve.sem_inc(S(f"mx_free{n % RB}"), 1)
                    dve.wait_ge(S("mx_full"), n + 2)
                    link(TT(tmp[:, g], mx(n + 1)[:, 0:NCP], st[:, g], ALU.mult))
                    dve.sem_inc(S(f"mx_free{(n + 1) % RB}"), 1)
                    link(TT(gi[:, g], gi[:, g], tmp[:, g], ALU.subtract))
                    link(dve.tensor_tensor_scan(gg[:, g], s5p[:, 13, GH * j + g:GH * j + g + 1].broadcast_to([P, NCP]),
                                                gi[:, g], 0.0, ALU.mult, ALU.add))
                dve.sem_inc(S("s5_g"), 1)
                link(dve.memset(hb[:, :, 0:1], 0.0))
                link(TT(gi, ct, gg, ALU.mult))
                for q in range(4):
                    n = b0 + 16 + q
                    dve.wait_ge(S("mx_full"), n + 1)
                    g2 = slice(2 * q, 2 * q + 2)
                    link(TT(tmp[:, g2], mx(n)[:, :].rearrange("p (g n) -> p g n", g=2), st[:, g2], ALU.mult))
                    dve.sem_inc(S(f"mx_free{n % RB}"), 1)
                link(TT(hb[:, :, 1:NCP], gi[:, :, 0:NCP - 1], tmp[:, :, 0:NCP - 1], ALU.add))
                dve.wait_ge(S("ld_u"), 16 * 9 * (j + 1))
                dve.sem_inc(S("s5_h"), 1)
                link(TT(hfin_p[:, gs], gi[:, :, NCP - 1], tmp[:, :, NCP - 1], ALU.add))
                n = b0 + 20
                dve.wait_ge(S("mx_full"), n + 1)
                hs = hfin_s[:, gs]
                sj = hfin[:, 208:272].rearrange("p (g b) -> p g b", g=GH)
                link(TT(sj, mx(n)[:, 0:64].rearrange("p (g b) -> p g b", g=GH), bc(pwi[:, CL, gs], NB), ALU.mult))
                dve.sem_inc(S(f"mx_free{n % RB}"), 1)
                link(TT(hs, hb[:, :, NCP:NC], bc(pwr[:, CL, gs], NB), ALU.mult))
                link(TT(hs, hs, sj, ALU.add))
                link(TT(hs, hs, ssm, ALU.add))
                dve.sem_inc(S("s5_fin"), 1)
                dve.wait_ge(S("s5_y"), j + 1)
                dve.wait_ge(S("st_y5"), 16 * CL * (j + 1))
                dve.wait_ge(S("st_mix"), ST_MIX[step])
                dve.sem_inc(S("mixer_done"), 1)

            def glu(step):
                dve.wait_ge(S("ld_glu"), 16 * 5)
                for j in range(2):
                    y, u = buf[j][:, 0:T], buf[2 + j][:, 0:T]
                    link(STT(y, u, V("s5_d", j), y, ALU.mult, ALU.add))
                dve.sem_inc(S("glu_y"), 1)
                dve.wait_ge(S("glu_done"), 1)
                for j in range(2):
                    o = buf[7 + j][:, 0:T].rearrange("p (n s) -> p s n", s=CL)
                    v = [buf[q][:, 0:T].rearrange("p (s n) -> p s n", s=CL) for q in (j, 2 + j)]
                    link(TT(o, v[0], v[1], ALU.mult))
                dve.sem_inc(S("mixer_done"), 1)

            def out(step):
                row = {"outA": 0, "outB": 2, "outC": 4}[step[0]]
                for c, (t0, w) in enumerate(CHUNKS):
                    n = base[step] + c
                    dve.wait_ge(S("mx_full"), n + 1)
                    link(TS(buf[2][:, t0:t0 + w], mx(n)[:, 0:w], 1.0 / W, EPS, ALU.mult, ALU.add))
                    dve.sem_inc(S(f"mx_free{n % RB}"), 1)
                dve.sem_inc(S("out_var"), 1)
                dve.wait_ge(S("out_sqrt"), OUTN[step[0]])
                link(dve.reciprocal(buf[2][:, 0:T], buf[2][:, 0:T]))
                for j in range(2):
                    link(STT(buf[3 + j][:, 0:T], buf[7 + j][:, 0:T], V("out_norm", row + j), buf[2][:, 0:T], ALU.mult, ALU.mult))
                dve.sem_inc(S("out_normed"), 1)
                dve.wait_ge(S("st_mixd"), 32 * OUTN[step[0]])
                dve.sem_inc(S("mixer_done"), 1)

            def qkv(step, i):
                if i == NT:
                    return
                r = rows(i)
                if i == 0:
                    dve.wait_ge(S("ld_qkvw"), 32)
                    link(TS(gain[:, 0:256], gain[:, 0:256], 0.125, None, ALU.mult))
                dve.wait_ge(S("qk_sq"), i + 1)
                link(dve.tensor_reduce(kss[0:r], ksq[0:r].rearrange("p (h e) -> p h e", e=64), AX.X, ALU.add))
                link(TS(kss[0:r], kss[0:r], 1.0 / 64, EPS, ALU.mult, ALU.add))
                dve.sem_inc(S("qk_ss"), 1)
                dve.wait_ge(S("qk_sqrt"), i + 1)
                link(dve.reciprocal(kss[0:r], kss[0:r]))
                if i >= 2:
                    dve.wait_ge(S(f"st_k{i % 2}"), 16 * (i // 2))
                    dve.wait_ge(S("qkT_ready"), i - 1)
                q = qks[0:r, i % 2]
                link(TT(q.rearrange("p (h e) -> p h e", e=64), bank[i % 2][0:r].rearrange("p (h e) -> p h e", e=64),
                        bc(kss[0:r], 64), ALU.mult))
                link(TT(q, q, gain[0:r], ALU.mult))
                dve.sem_inc(S("qk_ready"), 1)

            def att(step):
                dve.wait_ge(S("ld_t1"), 16 * 8)

                def smax(u):
                    ps = BLOCKS[u // 4][0]
                    w = 128 * len(BLOCKS[u // 4][4])
                    tab = (t2 if ps else t1)[:, u % 4]
                    if u % 4 == 0 and u >= 8:
                        dve.wait_ge(S(f"st_att{(u // 4) % 2}"), 16 * (u // 8))
                    if u >= 4:
                        dve.wait_ge(S("att_exp"), u - 3)
                    dve.wait_ge(S("att_s"), u + 1)
                    m = ost[:, (u // 4) % 2, u % 4, 64:65]
                    link(dve.tensor_tensor_reduce(out=ssb[:, u % 4, 0:w], in0=bank[u % 2][:, 0:w], in1=tab[:, tab.shape[1] - w:],
                                                  scale=1.0, scalar=-3e38, op0=ALU.add, op1=ALU.max, accum_out=m))
                    link(TS(nmax[:, u % 4:u % 4 + 1], m, -1.0, None, ALU.mult))
                    dve.sem_inc(S("att_max"), 1)

                def evac(u):
                    if u % 2 == 0:
                        w = 128 * len(BLOCKS[u // 4][4])
                        dve.wait_ge(S("att_pT"), u + 1)
                        if u >= 4:
                            dve.wait_ge(S("att_pv"), u - 3)
                        link(dve.tensor_copy(pt[:, u % 4, 0:w], bank[2 + u % 2][:, 0:w]))
                        dve.sem_inc(S("att_ptV"), 1)

                def outs(u):
                    if u % 4 == 3:
                        bk = u // 4
                        dve.wait_ge(S("att_pv"), u + 1)
                        link(dve.tensor_copy(ost[:, bk % 2, :, 0:64], bank[4 + bk % 2][:, 0:256].rearrange("p (h c) -> p h c", h=4)))
                        dve.sem_inc(S("att_o"), 1)
                for u in range(NU + 3):
                    if u < NU:
                        smax(u)
                    if 0 <= u - 1 < NU:
                        evac(u - 1)
                    if u >= 3:
                        outs(u - 3)

            def smp(step):
                link(dve.memset(qb, 0.0))
                for hp in range(2):
                    for hx in range(2):
                        rr = slice(64 * hx, 64 * hx + 64)
                        link(dve.tensor_copy(qb[rr, :, hp, 8 * (2 * hp + hx):8 * (2 * hp + hx) + 8],
                                             qkT[rr, hp, TP:T].rearrange("p (b s) -> p b s", b=NB)))
                dve.sem_inc(S("qb_ready"), 1)
                dve.wait_ge(S("ld_ts"), 16 * 16)
                dve.wait_ge(S("ld_vn"), 16 * 9)
                tb = ts[:, 0:2048].rearrange("p (m r) -> p r m", r=16)
                for hf in range(2):
                    dve.wait_ge(S("smp_s"), 4 * hf + 4)
                    if hf:
                        dve.wait_ge(S("smp_exp"), 1)
                    for q in range(2):
                        link(TT(sss[:, 512 * q:512 * q + 512].rearrange("p (r m) -> p r m", r=4),
                                bank[q][:, :].rearrange("p (r m) -> p r m", r=4), tb[:, 4 * q:4 * q + 4, :], ALU.add))
                    link(TT(sss[:, 1024:1280].rearrange("p (r m) -> p r m", r=8),
                            bank[2][:, 0:256].rearrange("p (r m) -> p r m", r=8), tb[:, 8:16, 96:128], ALU.add))
                    link(TT(sss[:, 1280:1288], bank[2][:, 256:264], ts[:, 2048:2056], ALU.add))
                    link(dve.tensor_reduce(sst[:, 0:1], sss, AX.X, ALU.max))
                    link(TS(sst[:, 1:2], sst[:, 0:1], -1.0, None, ALU.mult))
                    dve.sem_inc(S("smp_max"), 1)
                    dve.wait_ge(S("smp_pv"), 4 * hf + 4)
                    link(dve.reciprocal(sst[:, 3:4], sst[:, 2:3]))
                    v = sov.rearrange("p (h c) -> p h c", h=4)
                    link(TT(v, bank[6][:, 0:256].rearrange("p (h c) -> p h c", h=4), bc(hsel, 64), ALU.mult))
                    if hf:
                        dve.wait_ge(S("st_smp"), 16)
                    link(dve.tensor_reduce(so, sov.rearrange("p (h c) -> p c h", h=4), AX.X, ALU.add))
                    link(TS(so, so, sst[:, 3:4], None, ALU.mult))
                    dve.sem_inc(S("smp_o"), 1)

            def rows_(step):
                dve.wait_ge(S("ld_rows"), 16 * (1 + 3 + 24))
                for g, r in ((grow[0], P), (grow[1], 64)):
                    link(STT(g[0:r, 1], g[0:r, 1], 1.0, nrow[0:r], ALU.add, ALU.mult))

            def mrg(i):
                r = rows(i)
                o = od[0:r, i % 2]
                if i >= 2:
                    dve.wait_ge(S("odT_mm"), i - 1)
                if i < NT - 1:
                    dve.wait_ge(S(f"ld_ma{i % 2}"), 16 * (i // 2 + 1))
                    m = ma[:, i % 2]
                    mm_, d1, d2, e1, e2, den, w1, w2 = (mw[:, n] for n in (1, 2, 3, 4, 5, 6, 7, 8))
                    link(TT(mm_, m[:, 0, :, 64], m[:, 1, :, 64], ALU.max))
                    link(TT(d1, m[:, 0, :, 64], mm_, ALU.subtract))
                    link(TT(d2, m[:, 1, :, 64], mm_, ALU.subtract))
                    dve.sem_inc(S("mrg_d"), 1)
                    dve.wait_ge(S("mrg_e"), i + 1)
                    link(TT(w1, e1, m[:, 0, :, 65], ALU.mult))
                    link(TT(w2, e2, m[:, 1, :, 65], ALU.mult))
                    link(TT(den, w1, w2, ALU.add))
                    link(dve.reciprocal(den, den))
                    link(TT(w1, e1, den, ALU.mult))
                    link(TT(w2, e2, den, ALU.mult))
                    o3 = o.rearrange("p (h c) -> p h c", h=4)
                    link(TT(o3, m[:, 0, :, 0:64], bc(w1, 64), ALU.mult))
                    link(TT(osq.rearrange("p (h c) -> p h c", h=4), m[:, 1, :, 0:64], bc(w2, 64), ALU.mult))
                    link(TT(o, o, osq, ALU.add))
                else:
                    dve.wait_ge(S("ld_od"), 16 * NB)
                ss = mw[0:r, 9, 0:1]
                link(dve.tensor_tensor_reduce(out=osq[0:r], in0=o, in1=o, scale=1.0, scalar=0.0, op0=ALU.mult, op1=ALU.add, accum_out=ss))
                link(TS(ss, ss, 1.0 / W, EPS, ALU.mult, ALU.add))
                dve.sem_inc(S("mrg_ss"), 1)
                dve.wait_ge(S("mrg_sqrt"), i + 1)
                link(dve.reciprocal(ss, ss))
                link(TS(o, o, ss, None, ALU.mult))
                dve.sem_inc(S("mrg_o"), 1)

            def prj(i):
                r = rows(i)
                g = grow[i == NT - 1]
                dve.wait_ge(S(f"ld_xt{i % 2}"), 16 * (i // 2 + 1))
                if i >= 2:
                    dve.wait_ge(S(f"st_x1{i % 2}"), 16 * (i // 2))
                for q in range(2):
                    c = slice(512 * q, 512 * q + 512)
                    dve.wait_ge(S("prj_mm"), 2 * i + q + 1)
                    link(TT(x1[0:r, i % 2, c], bank[q][0:r], g[0:r, 0, c], ALU.mult))
                    dve.sem_inc(S("prj_free"), 1)
                link(TT(x1[0:r, i % 2], x1[0:r, i % 2], xt[0:r, i % 2], ALU.add))
                dve.sem_inc(S("x1_ready"), 1)

            def nrm(i):
                r = rows(i)
                g = grow[i == NT - 1]
                ss = mw[0:r, 10, 0:1]
                dve.wait_ge(S("x1_ss"), i + 1)
                link(TS(ss, ss, 1.0 / D, EPS, ALU.mult, ALU.add))
                dve.sem_inc(S("x1_var"), 1)
                dve.wait_ge(S("x1_sqrt"), i + 1)
                link(dve.reciprocal(ss, ss))
                if i >= 2:
                    dve.wait_ge(S(f"st_h2{i % 2}"), 16 * (i // 2))
                    dve.wait_ge(S("h2T_mm"), 2 * (i - 1))
                h = h2[0:r, i % 2]
                link(STT(h, x1[0:r, i % 2], ss, g[0:r, 1], ALU.mult, ALU.mult))
                link(TT(h, h, g[0:r, 2], ALU.add))
                dve.sem_inc(S("h2_ready"), 1)

            def route(step):
                g, e = lg[:, :, 0:4], lg[:, :, 4:36]
                link(dve.memset(lg[64:128, NT - 1], 0.0))
                dve.wait_ge(S("route_const"), 1)
                link(dve.tensor_copy(io32, io_i))
                link(dve.tensor_copy(blk0, blk_i))
                it4 = io32[:, 0:4].unsqueeze(1).broadcast_to([P, NT, 4])
                it32 = io32.unsqueeze(1).broadcast_to([P, NT, 32])
                m1, m2, gx = rs[:, 2, :, 0], rs[:, 2, :, 1], rs[:, 0, :, 0:4]
                oh1, oh2, em, t, R, tot = rt
                one4 = rs[:, 2, :, 4:8]

                def first_max(dst, src, mx_, iota, tmp, w):
                    link(dve.tensor_reduce(mx_, src, AX.X, ALU.max))
                    link(TT(tmp, src, bc(mx_, w), ALU.is_equal))
                    link(TT(tmp, tmp, iota, ALU.mult))
                    link(dve.tensor_reduce(rs[:, 2, :, 2], tmp, AX.X, ALU.min))
                    link(TT(dst, iota, bc(rs[:, 2, :, 2], w), ALU.is_equal))
                first_max(one4, g, m1, it4, gx, 4)
                link(TT(gx, g, bc(m1, 4), ALU.subtract))
                link(TS(rs[:, 1, :, 4:8], one4, 1e30, -1e30, ALU.mult, ALU.add))
                for q in range(4):
                    link(TT(em[:, :, 8 * q:8 * q + 8], e[:, :, 8 * q:8 * q + 8], bc(rs[:, 1, :, 4 + q], 8), ALU.add))
                first_max(oh1, em, m1, it32, t, 32)
                link(STT(em, oh1, -2e30, em, ALU.mult, ALU.add))
                first_max(oh2, em, m2, it32, t, 32)
                link(TT(rs[:, 1, :, 0], m2, m1, ALU.subtract))
                dve.sem_inc(S("rt_x"), 1)
                link(dve.memset(oh1[64:128, NT - 1], 0.0))
                link(dve.memset(oh2[64:128, NT - 1], 0.0))
                link(TT(em, oh1, oh2, ALU.add))
                dve.sem_inc(S("rt_oh"), 1)
                emf, Rf, totf = (v.rearrange("p i e -> p (i e)") for v in (em, R, tot))
                dve.wait_ge(S("rt_mm"), 1)
                link(dve.tensor_copy(Rf[:, 0:512], bank[0][:, :]))
                link(dve.tensor_copy(Rf[:, 512:544], bank[1][:, 0:32]))
                link(dve.tensor_copy(totf[:, 0:512], bank[2][:, :]))
                link(dve.tensor_copy(totf[:, 512:544], bank[3][:, 0:32]))
                cnt, pad, ends, bs, on = (re_[:, n] for n in range(5))
                link(dve.memset(cnt, 0.0))
                link(dve.memset(on, 1.0))
                for i in range(NT):
                    link(TT(R[:, i], R[:, i], cnt, ALU.add))
                    link(TT(cnt, cnt, tot[:, i], ALU.add))
                link(TS(pad, cnt, 1.0 / MOEB, (MOEB - 1.0) / MOEB - (MOEB - 1.0) / (2 * MOEB), ALU.mult, ALU.add))
                link(TS(pad, pad, 12582912.0, None, ALU.add))
                link(TS(pad, pad, 12582912.0, float(MOEB), ALU.subtract, ALU.mult))
                link(dve.tensor_tensor_scan(ends, on, pad, 0.0, ALU.mult, ALU.add))
                link(TT(bs, ends, pad, ALU.subtract))
                link(TT(R, R, bs.unsqueeze(1).broadcast_to([P, NT, 32]), ALU.add))
                for k, oh in enumerate((oh1, oh2)):
                    link(TT(t, oh, R, ALU.mult))
                    link(dve.tensor_reduce(rs[:, 2, :, 2], t, AX.X, ALU.add))
                    link(dve.tensor_copy(dest[:, :, k], rs[:, 2, :, 2]))
                dve.sem_inc(S("dest_ready"), 1)
                def over(ap):
                    return ap[0:1].unsqueeze(1).broadcast_to([1, NSUB, 32])
                link(TT(cmpb[0:1], over(ends), bc(blk0[0:1], 32), ALU.is_le))
                link(dve.tensor_reduce(zsum[0:1], cmpb[0:1], AX.X, ALU.add))
                link(TS(zsum[0:1], zsum[0:1], float(NE - 1), None, ALU.min))
                link(dve.tensor_copy(bexp[0:1], zsum[0:1].rearrange("p (b two) -> p b two", two=2)[:, :, 0]))
                link(TT(cnt, cnt, bs, ALU.add))
                link(TT(cmpb[0:1], over(bs), bc(blk0[0:1], 32), ALU.is_le))
                link(TT(cmpc[0:1], over(cnt), bc(blk0[0:1], 32), ALU.is_gt))
                link(TT(cmpb[0:1], cmpb[0:1], cmpc[0:1], ALU.mult))
                link(dve.tensor_reduce(zsum[0:1], cmpb[0:1], AX.X, ALU.add))
                link(dve.tensor_copy(used[0:1], zsum[0:1]))
                dve.sem_inc(S("route_done"), 1)
                dve.wait_ge(S("rt_e"), 1)
                gp, ex, p1 = rs[:, 2, :, 0], rs[:, 1, :, 0], rs[:, 1, :, 1]
                link(dve.tensor_reduce(gp, gx, AX.X, ALU.add))
                link(dve.reciprocal(gp, gp))
                link(TS(p1, ex, 1.0, None, ALU.add))
                link(dve.reciprocal(p1, p1))
                link(TT(gate[:, :, 0], p1, gp, ALU.mult))
                link(TT(gate[:, :, 1], gate[:, :, 0], ex, ALU.mult))

            def moe(step):
                def xt_half(b, s, u):
                    def work():
                        dve.wait_ge(S("xT_mm"), b * 2 + 1)
                        dve.tensor_copy(xgT[:, s, 0:4], bank[0][:, :].rearrange("p (k t) -> p k t", k=4)).then_inc(S("xtV"), 1)
                    if_used(dve, u, work, [("xtV", b, 1)])

                def sub(it, q, u):
                    b, s = it * 4 + q, q % 2
                    first = isinstance(b, int) and b < 2
                    last = isinstance(it, int) and it == LAST

                    def hidden():
                        dve.wait_ge(S("silu"), b + 1)
                        dve.wait_ge(S("u_mm"), b + 1)
                        TT(hh, gs, bank[3][:, :], ALU.mult).then_inc(S("h_ready2"), 1)
                        dve.wait_ge(S("hT_mm"), b + 1)
                        dve.tensor_copy(hhT, bank[6][:, :].rearrange("p (k t) -> p k t", k=4)).then_inc(S("hT_ready"), 1)
                    if_used(dve, u, hidden, [("h_ready2", b, 1), ("hT_ready", b, 1)])
                    if not (last and q >= 2):
                        xt_half(b + 2, s, flag(dve, b + 2))

                    def work():
                        dve.wait_ge(S("y_mm"), b + 1)
                        if not first:
                            dve.wait_ge(S(f"st_ye{s}"), it * 32 + 16 * (q // 2))
                        dve.tensor_copy(yb[:, s, 0:512], bank[4][:, :]).then_inc(S("yV"), 1)
                    if_used(dve, u, work, [("yV", b, 1)])
                xt_half(0, 0, None)
                xt_half(1, 1, flag(dve, 1))
                quads(dve, sub, lambda it: [("h_ready2", it * 4, 4), ("hT_ready", it * 4, 4), ("xtV", it * 4 + 2, 4), ("yV", it * 4, 4)])

            def comb(step):
                dve.wait_ge(S("ld_g2"), 16 * 9)
                for q in range(NT):
                    r = rows(q)
                    g = g2r[0:r, int(q == NT - 1)]
                    dve.wait_ge(S(f"ld_cy{q % 4}"), 32 * (q // 4 + 1))
                    dve.wait_ge(S(f"ld_cx{q % 4}"), 16 * (q // 4 + 1))
                    y1, y2 = cy[0:r, q % 4, 0], cy[0:r, q % 4, 1]
                    link(TS(y1, y1, gate[0:r, q, 0:1], None, ALU.mult))
                    link(STT(y1, y2, gate[0:r, q, 1:2], y1, ALU.mult, ALU.add))
                    link(TT(y1, y1, g, ALU.mult))
                    link(TT(cx[0:r, q % 4], cx[0:r, q % 4], y1, ALU.add))
                    dve.sem_inc(S("comb_done"), 1)

            run({"s5par": s5par, "norm1": norm1, "A": lru, "B": sconv, "s5prep": s5prep, "s5": s5, "glu": glu,
                 "outA": out, "outB": out, "outC": out, "qkv": qkv, "bar": barrier(dve), "att": att, "smp": smp,
                 "rows": rows_, "row": parts((nrm, 2), (mrg, 0), (prj, 1)), "route": route, "moe": moe, "comb": comb})

        @block.tensor
        def _(pe):
            mm = pe.matmul

            def mod(step):
                pe.wait_ge(S("ones_ready"), 1)
                pe.wait_ge(S("c_silu"), 1)
                for n in range(12):
                    pe.wait_ge(S(f"ld_modw{n % 4}"), 16 * (n // 4 + 1))
                    if n >= 2:
                        pe.wait_ge(S("mod_row"), n - 1)
                    o = bank[n % 2][0:9, :]
                    for k in range(KT):
                        mm(o, cS[:, k, :], modw[:, n % 4, k, :], start=(k == 0), stop=False)
                    mm(o, ones[0:1, 0:9], modb[0:1, n * 512:(n + 1) * 512], start=False, stop=True).then_inc(S("mod_mm"), 1)
                pe.wait_ge(S("mod_row"), 12)
                for k in range(16):
                    ins = pe.transpose(bank[2][:, 9 * k:9 * k + 9], modrow[0:9, k * P:(k + 1) * P], ident[0:9, 0:9])
                ins.then_inc(S("modT_mm"), 1)

            def norm1(step):
                for c, (t0, w) in enumerate(CHUNKS):
                    if c:
                        pe.wait_ge(S("norm1_var"), c)
                    for k in range(KT):
                        n = c * KT + k
                        pe.wait_ge(S("norm1_sq"), n + 1)
                        mm(bank[0][:, 0:w], ones, sq1[:, n % 2, 0:w], start=(k == 0), stop=(k == KT - 1)).then_inc(S("norm1_mm"), 1)

            def z(step, i):
                pe.wait_ge(S(f"ld_wz{i % 3}"), 16 * (i // 3 + 1))
                if i == 0:
                    pe.wait_ge(S("h_ready"), 4)
                    pe.wait_ge(S("hs_ready"), 1)
                    pe.wait_ge(S("modT_ready"), 1)
                for c, (t0, w) in enumerate(CHUNKS):
                    n = 5 * i + c
                    if n >= 2:
                        pe.wait_ge(S("z_free"), n - 1)
                    for k in range(KT):
                        ins = mm(bank[n % 2][:, 0:w], wz[:, i % 3, k, :], hT[:, k, t0:t0 + w], start=(k == 0), stop=(k == KT - 1))
                    ins.then_inc(S("z_mm"), 1)

            def lru(step, j):
                pe.wait_ge(S("lru_y"), j + 1)
                pe.wait_ge(S("ld_gatew"), 16)
                for q in range(2):
                    for c, (t0, w) in enumerate(CHUNKS):
                        n = base[step] + 5 * q + c
                        mx_take(pe, n)
                        mm(mx(n)[:, 0:w], gatew[:, 2 * q + j, :], buf[1][:, t0:t0 + w], start=True, stop=True).then_inc(S("mx_full"), 1)

            def s5prep(step, j):
                b0 = base[step]
                pe.wait_ge(S("s5_ff"), j + 1)
                for q in range(GH):
                    if q % 4 == 0:
                        mx_take(pe, b0 + q // 4)
                    ins = mm(mx(b0 + q // 4)[0:16, (q % 4) * P:(q % 4 + 1) * P], s5b[:, 0, GH * j + q, :],
                             ff[:, q, 0:CL, :], start=True, stop=True)
                    if q % 4 == 3:
                        ins.then_inc(S("mx_full"), 1)
                pe.wait_ge(S("s5_et"), j + 1)
                for q in range(GH):
                    n = b0 + 2 + q // 4
                    if q % 4 == 0:
                        mx_take(pe, n)
                    ins = pe.transpose(mx(n)[:, (q % 4) * P:(q % 4 + 1) * P], buf[0][:, q * P:(q + 1) * P], ident)
                    if q % 4 == 3:
                        ins.then_inc(S("mx_full"), 1)

            def s5(step, j):
                b0 = base[step]
                pe.wait_ge(S("mixer_done"), ORD[step])
                pe.wait_ge(S("ld_u"), 16 * 9 * (j + 1))
                ub = buf[0][:, 0:GH * NC].rearrange("p (g n) -> p g n", g=GH)
                hb = buf[5][:, 0:GH * NC].rearrange("p (g n) -> p g n", g=GH)
                gg = buf[4][:, 0:GH * NCP].rearrange("p (g n) -> p g n", g=GH)
                for g in range(GH):
                    for q, e in enumerate((emat, emat2)):
                        n = b0 + 2 * g + q
                        mx_take(pe, n)
                        mm(mx(n)[:, 0:NC], e[:, g, :], ub[:, g, :], start=True, stop=True).then_inc(S("mx_full"), 1)
                pe.wait_ge(S("s5_g"), j + 1)
                for q in range(4):
                    n = b0 + 16 + q
                    mx_take(pe, n)
                    mm(mx(n), jmat, gg[:, 2 * q:2 * q + 2, :], start=True, stop=True).then_inc(S("mx_full"), 1)
                n = b0 + 20
                mx_take(pe, n)
                mm(mx(n)[:, 0:64], jmat, hb[:, :, NCP:NC], start=True, stop=True).then_inc(S("mx_full"), 1)
                pe.wait_ge(S("s5_h"), j + 1)
                pe.wait_ge(S("toep_ready"), 16 * CL * (j + 1))
                for g in range(GH):
                    n = b0 + 21 + g
                    mx_take(pe, n)
                    mm(mx(n)[:, 0:NC], toep[:, g, :], ub[:, g, :], start=True, stop=False)
                    mm(mx(n)[:, 0:NC], ff[:, g, 1:CL + 1, :], hb[:, g, :], start=False, stop=True).then_inc(S("mx_full"), 1)

            def glu(step):
                pe.wait_ge(S("glu_gelu"), 1)
                pe.wait_ge(S("ld_glu"), 16 * 5)
                gw = buf[6][:, 0:1024].rearrange("p (k m) -> p k m", k=2)
                for m in range(4):
                    for c, (t0, w) in enumerate(CHUNKS):
                        n = base[step] + 5 * m + c
                        mx_take(pe, n)
                        for k in range(2):
                            ins = mm(mx(n)[:, 0:w], gw[:, k, m * P:(m + 1) * P], buf[4 + k][:, t0:t0 + w], start=(k == 0), stop=(k == 1))
                        ins.then_inc(S("mx_full"), 1)

            def out(step):
                pe.wait_ge(S("out_sq"), OUTN[step[0]])
                for c, (t0, w) in enumerate(CHUNKS):
                    n = base[step] + c
                    mx_take(pe, n)
                    for j in range(2):
                        ins = mm(mx(n)[:, 0:w], ones, buf[j][:, t0:t0 + w], start=(j == 0), stop=(j == 1))
                    ins.then_inc(S("mx_full"), 1)

            def qkv(step, i):
                if i < NT:
                    r, t0 = rows(i), i * P
                    if i == 0:
                        pe.wait_ge(S("ld_qkvw"), 32)
                        pe.wait_ge(S("z_free"), 60)
                    if i >= 2:
                        pe.wait_ge(S("qk_ready"), i - 1)
                    for k in range(KT):
                        mm(bank[i % 2][0:r], hT[:, k, t0:t0 + r], wqkv[:, k, 0:512], start=(k == 0), stop=(k == KT - 1))
                    if i >= 1:
                        pe.wait_ge(S("v_free"), i)
                    for k in range(KT):
                        ins = mm(bank[7][0:r, 0:256], hT[:, k, t0:t0 + r], wqkv[:, k, 512:768], start=(k == 0), stop=(k == KT - 1))
                    ins.then_inc(S("v_mm"), 1)
                if i:
                    r = rows(i - 1)
                    n = base[step]
                    pe.wait_ge(S("qk_ready"), i)
                    mx_take(pe, n)
                    for q in range(4):
                        ins = pe.transpose(mx(n)[:, q * P:q * P + r], qks[0:r, (i - 1) % 2, q * P:(q + 1) * P], ident[0:r, 0:r])
                    ins.then_inc(S("mx_full"), 1)

            def tab(step):
                pe.wait_ge(S("ld_tab"), 32)
                for c in range(7):
                    w = min(512, L1 + L2 + L3 - 512 * c)
                    mm(bank[c][0:4, 0:w], rbx[0:33], tabc[0:33, 512 * c:512 * c + w], start=True, stop=True).then_inc(S("tab_mm"), 1)

            def att(step):
                pe.wait_ge(S("ld_qkT"), 16)
                pe.wait_ge(S("ld_v1"), 16)
                pe.wait_ge(S("ld_v2"), 64)

                def scores(u):
                    ps, n, q, k, vt = BLOCKS[u // 4]
                    h = u % 4
                    rr = slice(64 * (h % 2), 64 * (h % 2) + 64)
                    if u >= 2:
                        pe.wait_ge(S("att_max"), u - 1)
                    mm(bank[u % 2][:, 0:128 * len(vt)], qkT[rr, h // 2, q], qkT[rr, 2 + h // 2, k], start=True, stop=True).then_inc(S("att_s"), 1)

                def turn(u):
                    vt = BLOCKS[u // 4][4]
                    pe.wait_ge(S("att_exp"), u + 1)
                    if u >= 2:
                        pe.wait_ge(S("att_ptA" if u % 2 else "att_ptV"), u // 2)
                    for c in range(len(vt)):
                        ins = pe.transpose(bank[2 + u % 2][:, c * P:(c + 1) * P], pp[:, u % 4, c * P:(c + 1) * P], ident)
                    ins.then_inc(S("att_pT"), 1)

                def pv(u):
                    ps, n, q, k, vt = BLOCKS[u // 4]
                    h, bk = u % 4, u // 4
                    v = v2 if ps else v1
                    pe.wait_ge(S("att_ptA" if u % 2 else "att_ptV"), u // 2 + 1)
                    if h == 0 and bk >= 2:
                        pe.wait_ge(S("att_o"), bk - 1)
                    for c, t in enumerate(vt):
                        ins = mm(bank[4 + bk % 2][:, 64 * h:64 * h + 64], pt[:, u % 4, c * P:(c + 1) * P], v[:, t, 64 * h:64 * h + 64],
                                 start=(c == 0), stop=(c == len(vt) - 1))
                    ins.then_inc(S("att_pv"), 1)
                for u in range(NU + 3):
                    if u < NU:
                        scores(u)
                    if 0 <= u - 1 < NU:
                        turn(u - 1)
                    if 0 <= u - 2 < NU:
                        pv(u - 2)

            def smp(step):
                pe.wait_ge(S("qb_ready"), 1)
                pe.wait_ge(S("att_o"), len(BLOCKS))
                pe.wait_ge(S("ld_vn"), 16 * 9)
                for hf in range(2):
                    for b4 in range(4):
                        b = 4 * hf + b4
                        pe.wait_ge(S(f"ld_kc{b % 2}"), 16 * (b // 2 + 1))
                        if hf and b4 == 0:
                            pe.wait_ge(S("smp_max"), 1)
                        rr = slice(32 * b4, 32 * b4 + 32)
                        for c, (c0, w) in enumerate(((0, 512), (512, 512), (1024, 256))):
                            for hp in range(2):
                                mm(bank[c][rr, 0:w], qb[:, b, hp, :], kc[:, b % 2, hp, c0:c0 + w], start=(hp == 0), stop=(hp == 1),
                                   tile_position=(0, 32 * b4))
                        for hp in range(2):
                            ins = mm(bank[2][rr, 256:264], qb[:, b, hp, :], qkT[:, 2 + hp, TP + 8 * b:TP + 8 * b + 8],
                                     start=(hp == 0), stop=(hp == 1), tile_position=(0, 32 * b4))
                        ins.then_inc(S("smp_s"), 1)
                    pe.wait_ge(S("smp_exp"), hf + 1)
                    for q in range(3):
                        if hf:
                            pe.wait_ge(S("smp_pt"), 3)
                        for c in range(4 if q < 2 else 2):
                            ins = pe.transpose(bank[3 + q][:, c * P:(c + 1) * P], spp[:, (4 * q + c) * P:(4 * q + c + 1) * P], ident)
                        if q == 2:
                            ins = pe.transpose(bank[5][0:8, 2 * P:3 * P], spp[:, 1280:1288], ident)
                        ins.then_inc(S("smp_pT"), 1)
                    pe.wait_ge(S("smp_pt"), 3 * hf + 3)
                    if hf:
                        pe.wait_ge(S("smp_o"), 1)
                    for b4 in range(4):
                        b = 4 * hf + b4
                        rr = slice(32 * b4, 32 * b4 + 32)
                        pe.wait_ge(S(f"ld_vc{b % 2}"), 16 * (b // 2 + 1))
                        for c in range(10):
                            mm(bank[6][rr, 0:256], spt[:, c, rr], vc[:, b % 2, c, :], start=(c == 0), stop=False, tile_position=(0, 32 * b4))
                        mm(bank[6][rr, 0:256], spt[0:8, 10, rr], vn[0:8, b], start=False, stop=True,
                           tile_position=(0, 32 * b4)).then_inc(S("smp_pv"), 1)

            def mrg(i):
                r = rows(i)
                pe.wait_ge(S("mrg_o"), i + 1)
                if i >= 1:
                    pe.wait_ge(S("odT_ready"), i)
                for k in range(2):
                    ins = pe.transpose(bank[4][:, k * P:k * P + r], od[0:r, i % 2, k * P:(k + 1) * P], ident[0:r, 0:r])
                ins.then_inc(S("odT_mm"), 1)

            def prj(i):
                r = rows(i)
                pe.wait_ge(S(f"ld_mix{i % 3}"), 16 * (i // 3 + 1))
                pe.wait_ge(S("ld_wo"), 48)
                pe.wait_ge(S("odT_ready"), i + 1)
                for q in range(2):
                    if i:
                        pe.wait_ge(S("prj_free"), 2 * i - 1 + q)
                    for k in range(KT):
                        l = mixl[:, i % 3, k, 0:r] if k < 6 else odt[:, i % 2, k - 6, 0:r]
                        ins = mm(bank[q][0:r], l, wo[:, k, 512 * q:512 * q + 512], start=(k == 0), stop=(k == KT - 1))
                    ins.then_inc(S("prj_mm"), 1)

            def turn_h2(i):
                r = rows(i)
                pe.wait_ge(S("h2_ready"), i + 1)
                if i:
                    pe.wait_ge(S("h2T_ready"), i)
                for q in range(2):
                    for k in range(4):
                        kk = 4 * q + k
                        ins = pe.transpose(bank[2 + q][:, k * P:k * P + r], h2[0:r, i % 2, kk * P:(kk + 1) * P], ident[0:r, 0:r])
                    ins.then_inc(S("h2T_mm"), 1)

            def logits(i):
                r = rows(i)
                pe.wait_ge(S("h2T_ready"), i + 1)
                if i:
                    pe.wait_ge(S("lg_free"), i)
                for k in range(KT):
                    mm(bank[5][0:r, 0:36], h2T[:, i % 2, k, 0:r], rw[:, k, :], start=(k == 0), stop=False)
                mm(bank[5][0:r, 0:36], ones[0:1, 0:r], rb[0:1, :], start=False, stop=True).then_inc(S("lg_mm"), 1)

            def route(step):
                pe.wait_ge(S("rt_oh"), 1)
                pe.wait_ge(S("route_const"), 1)
                mf = rt[2].rearrange("p i e -> p (i e)")
                mm(bank[0][:, :], tri, mf[:, 0:512], start=True, stop=True)
                mm(bank[1][:, 0:32], tri, mf[:, 512:544], start=True, stop=True)
                mm(bank[2][:, :], ones, mf[:, 0:512], start=True, stop=True)
                mm(bank[3][:, 0:32], ones, mf[:, 512:544], start=True, stop=True).then_inc(S("rt_mm"), 1)

            def moe(step):
                pe.wait_ge(S("route_done"), 1)

                def turn(it, q, u):
                    s = q % 2
                    x = xg[:, s].rearrange("p (q k) -> p k q", k=KT)

                    def work():
                        pe.wait_ge(S(f"ld_xg{s}"), it * 32 + 16 * (q // 2) + 16)
                        for h in range(2):
                            for k in range(4):
                                ins = pe.transpose(bank[h][:, k * P:(k + 1) * P], x[:, 4 * h + k, :], ident)
                            ins.then_inc(S("xT_mm"), 1)
                    if_used(pe, u, work, [("xT_mm", (it * 4 + q) * 2, 2)])

                def up(w, bk, sem, it, q, u):
                    b, s, ws = it * 4 + q, q % 2, q // 2

                    def work():
                        pe.wait_ge(S("xtA"), b + 1)
                        pe.wait_ge(S("xtV"), b + 1)
                        pe.wait_ge(S(f"ld_{sem}{ws}"), it * 16 + 16)
                        if sem == "g_mm" and not (isinstance(b, int) and b == 0):
                            pe.wait_ge(S("silu"), b)
                        for k in range(KT):
                            ins = mm(bank[bk][:, :], xgT[:, s, k, :], w[:, ws, k, :], start=(k == 0), stop=(k == KT - 1))
                        ins.then_inc(S(sem), 1)
                    if_used(pe, u, work, [(sem, b, 1)])

                def after(it, q, n):
                    return (it, q + n) if q + n < 4 else (it + 1, q + n - 4)

                def sub(it, q, u):
                    b, ws = it * 4 + q, q // 2
                    first = isinstance(b, int) and b == 0
                    last = isinstance(it, int) and it == LAST
                    up(wu, 3, "u_mm", it, q, u)
                    if not (last and q == 3):
                        up(wg, 2, "g_mm", *after(it, q, 1), flag(pe, b + 1))

                    def hturn():
                        hq = hh.rearrange("p (q k) -> p k q", k=4)
                        pe.wait_ge(S("h_ready2"), b + 1)
                        for k in range(4):
                            ins = pe.transpose(bank[6][:, k * P:(k + 1) * P], hq[:, k, :], ident)
                        ins.then_inc(S("hT_mm"), 1)
                    if_used(pe, u, hturn, [("hT_mm", b, 1)])
                    if not (last and q >= 2):
                        turn(*after(it, q, 2), flag(pe, b + 2))

                    def down():
                        pe.wait_ge(S("hT_ready"), b + 1)
                        pe.wait_ge(S(f"ld_y_mm{ws}"), it * 16 + 16)
                        if not first:
                            pe.wait_ge(S("yA"), b)
                            pe.wait_ge(S("yV"), b)
                        for h in range(2):
                            for k in range(4):
                                ins = mm(bank[4 + h][:, :], hhT[:, k, :], wd[:, ws, k, 512 * h:512 * h + 512], start=(k == 0), stop=(k == 3))
                        ins.then_inc(S("y_mm"), 1)
                    if_used(pe, u, down, [("y_mm", b, 1)])
                turn(0, 0, None)
                up(wg, 2, "g_mm", 0, 0, None)
                turn(0, 1, flag(pe, 1))
                quads(pe, sub, lambda it: [("u_mm", it * 4, 4), ("g_mm", it * 4 + 1, 4), ("hT_mm", it * 4, 4),
                                           ("xT_mm", it * 8 + 4, 8), ("y_mm", it * 4, 4)])

            run({"mod": mod, "norm1": norm1, "z": z, "A": lru, "s5prep": s5prep, "s5": s5, "glu": glu,
                 "outA": out, "outB": out, "outC": out, "qkv": qkv, "bar": barrier(pe), "tab": tab, "att": att, "smp": smp,
                 "row": parts((prj, 1), (logits, 3), (mrg, 0), (turn_h2, 2)), "route": route, "moe": moe})


def _bucket(n):
    n = np.asarray(n).astype(np.int32)
    nf = np.maximum(n, 1).astype(np.float32)
    large = 16 + (np.log(nf / 16) / np.log(2048 / 16) * 16).astype(np.int32)
    return np.where(n < 16, n, np.minimum(large, BK - 1)).astype(np.int32)


def _table_constants():
    near = lambda d: (d >= 0) & (d <= 128)
    mid = lambda d: (d >= 0) & (d % 4 == 0) & (d <= 512)
    far = lambda d: (d >= 0) & (d % 16 == 0) & (d <= 2048)
    d1 = 255 - np.arange(L1)
    d2 = 4 * (511 - np.arange(L2))
    d3 = 2055 - np.arange(L3)
    out = []
    for d, n in ((d1, near(d1) * 1), (d2, mid(d2) * 1 + far(d2)), (d3, near(d3) * 1 + mid(d3) + far(d3))):
        oh = (np.arange(BK)[:, None] == _bucket(np.clip(d, 0, None))[None]) * (n > 0)
        add = np.where(n > 0, np.log(np.maximum(n, 1)), NEG)
        out.append(np.concatenate([oh, add[None]], axis=0))
    return np.concatenate(out, axis=1).astype(np.float32)


_OUT_SHAPES = {
    "y": (T, D), "k": (T, 256), "v": (T, 256),
    "p_lru_h": (256, 1), "s_lru_h": (256, 8), "p_lru_conv": (256, 3), "s_lru_conv": (256, 8, 3),
    "p_sconv": (256, 2), "s_sconv": (256, 8, 2), "p_s5": (P, 16), "s_s5": (P, 16, 8),
}


def _columns(v):
    return np.asarray(v).reshape(-1, P).T


def layout(i):
    f = {}
    x = np.concatenate([i["x_prompt"][0], i["x_sample"].reshape(NB * NS, D)], axis=0)
    f["xT"] = x.T.reshape(KT, P, T).transpose(1, 0, 2)
    c = np.concatenate([i["c_prompt"], i["c_sample"]], axis=0)
    f["cT"] = c.T.reshape(KT, P, 9).transpose(1, 0, 2)
    f["mod_w"] = i["mod_w"][0].reshape(KT, P, 12, 512).transpose(2, 1, 0, 3)
    f["mod_b"] = i["mod_b"]
    w = i["w_in"][0].reshape(KT, P, 9, 2, P)
    slices = {XA: 0, GA: 1, GB: 2, GC: 3, XB: 4, UC: 5}
    f["w_z"] = np.stack([w[:, :, slices[s], h].transpose(1, 0, 2) for s, h in ZTILES])
    two = lambda v: np.asarray(v)[0].reshape(-1, 2, P).transpose(2, 1, 0).reshape(P, -1)
    half = lambda v: np.asarray(v)[0].reshape(2, P).T
    vec = [_columns(i["norm_mix"][0]), two(i["lru_conv_w"]), half(i["lru_conv_b"]), half(i["lru_ba"]), half(i["lru_bx"]),
           half(i["lru_lambda"]), two(i["sconv_w"]), half(i["s5_d"]), _columns(i["s5_glu_b"][0]), _columns(i["out_norm"][0]),
           i["state_lru_h"][0].reshape(NB, 2, P).transpose(2, 1, 0).reshape(P, 16),
           i["state_lru_conv"][0].reshape(NB, 3, 2, P).transpose(3, 2, 0, 1).reshape(P, 48),
           i["state_sconv"][0].reshape(NB, 2, 2, P).transpose(3, 2, 0, 1).reshape(P, 32),
           np.repeat(np.array([-1.0, 1.0], np.float32), 64)[:, None]]
    f["vec"] = np.concatenate(vec, axis=1)
    f["ident"] = np.eye(P, dtype=np.float32)
    jm = np.zeros((P, P), np.float32)
    jm[np.arange(64) + 64, np.arange(64)] = -1.0
    jm[np.arange(64), np.arange(64) + 64] = 1.0
    f["jmat"] = jm
    gw = np.zeros((P, 4, P), np.float32)
    for q, name in enumerate(("lru_wa", "lru_wx")):
        for h in range(4):
            s = slice(64 * (h % 2), 64 * (h % 2) + 64)
            gw[s, 2 * q + h // 2, s] = i[name][0, h]
    f["gatew"] = gw
    st = lambda v: np.concatenate([v[0].T, v[0].T], axis=0)
    f["s5p"] = np.stack([st(i["s5_a_re"]), st(i["s5_a_im"]), np.broadcast_to(i["s5_log_dt"][0], (P, G16))], axis=1)
    br, bi = (i[n][0].transpose(1, 0, 2) for n in ("s5_b_re", "s5_b_im"))
    cr, ci = (i[n][0].transpose(2, 0, 1) for n in ("s5_c_re", "s5_c_im"))
    f["s5b"] = np.stack([np.concatenate(p, axis=0) for p in ((br, bi), (bi, br), (cr, ci), (ci, cr))], axis=1)
    f["s5_0"] = np.concatenate([i[n][0].transpose(2, 1, 0) for n in ("state_s5_re", "state_s5_im")], axis=0)
    f["glu_w"] = i["s5_glu_w"][0].reshape(2, P, 512).transpose(1, 0, 2).reshape(P, 1024)
    f["x"] = x
    f["w_qkv"] = i["w_in"][0].reshape(KT, P, 2304)[:, :, 1536:].transpose(1, 0, 2)
    f["qk_gain"] = np.broadcast_to(np.concatenate([np.tile(i["q_norm"][0], 4), np.tile(i["k_norm"][0], 4)]), (P, 512))
    f["tabc"] = _table_constants()
    f["rbx"] = np.concatenate([i["rel_bias"], np.ones((1, 4), np.float32)], axis=0)
    f["hsel"] = np.tile(np.repeat(np.eye(4, dtype=np.float32), 8, axis=0), (4, 1))
    def cache(v):
        v = v[0].reshape(NB, 128, 16, 4, 64).transpose(0, 2, 1, 3, 4)
        return np.concatenate([v[:, :8].reshape(NB, 1024, 4, 64), v[:, 8:, 96:].reshape(NB, 256, 4, 64)], axis=1)
    f["kc"] = cache(i["cache_win_k"]).reshape(NB, 1280, 2, P).transpose(0, 3, 2, 1)
    f["vc"] = cache(i["cache_win_v"]).reshape(NB, 10, P, 256).transpose(0, 2, 1, 3)
    f["w_out"] = i["w_out"][0].reshape(KT, P, D).transpose(1, 0, 2)
    f["rw"] = np.concatenate([i["router_g_w"][0], i["router_e_w"][0]], axis=1).reshape(KT, P, 36).transpose(1, 0, 2)
    f["rb"] = np.concatenate([i["router_g_b"][0], i["router_e_b"][0]])[None]
    f["nffn"] = i["norm_ffn"]
    f["wg"] = i["moe_w_gate"][0].reshape(NE, P, KT * DE)
    f["wu"] = i["moe_w_up"][0].reshape(NE, P, KT * DE)
    f["wd"] = i["moe_w_down"][0].reshape(NE, P, 4 * D)
    return {n: np.ascontiguousarray(v) for n, v in f.items()}


def kernel(**inputs):
    import concourse.bacc as bacc
    from concourse.bass_utils import run_bass_kernel_spmd

    nc = bacc.Bacc("TRN2", target_bir_lowering=False, num_devices=1)
    arrays = layout({n: np.asarray(v) for n, v in inputs.items()})
    A = {n: nc.dram_tensor(n, a.shape, mybir.dt.from_np(a.dtype), kind="ExternalInput").ap() for n, a in arrays.items()}
    O = {n: nc.dram_tensor("o_" + n, s, F32, kind="ExternalOutput").ap() for n, s in _OUT_SHAPES.items()}
    build(nc, A, O)
    r = run_bass_kernel_spmd(nc, [arrays], core_ids=[0]).results[0]
    g = {n: r["o_" + n] for n in _OUT_SHAPES}
    return finish(g)


def finish(g):
    f = lambda v: np.ascontiguousarray(v)[None]
    z = np.zeros
    p5, s5 = g["p_s5"], g["s_s5"]
    return (g["y"][:TP].reshape(1, TP, D), g["y"][TP:].reshape(NB, NS, D),
            f(g["p_lru_h"].T), f(g["p_lru_conv"].T[None]), f(g["p_sconv"].T[None]),
            f(p5[:64].T[None]), f(p5[64:].T[None]), g["k"][:TP].reshape(1, 1, TP, 4, 64), g["v"][:TP].reshape(1, 1, TP, 4, 64),
            f(g["s_lru_h"].T), f(g["s_lru_conv"].transpose(1, 2, 0)), f(g["s_sconv"].transpose(1, 2, 0)),
            f(s5[:64].transpose(2, 1, 0)), f(s5[64:].transpose(2, 1, 0)),
            g["k"][TP:].reshape(1, NB, NS, 4, 64), g["v"][TP:].reshape(1, NB, NS, 4, 64))
```
